# Optimizing a Trainium2 kernel written in Bass

```python
import math
import jax, jax.numpy as jnp
from jax import lax
import numpy as np

D_MODEL = 1024
BATCH = 1
SEQ = 512
DEPTH = 2

EPS = 1e-6
N_MEM = 256
HEAD_DIM = 64
X_HEADS = 4
X_WIDTH = X_HEADS * HEAD_DIM
MIX_WIDTH = D_MODEL
TM_WIDTH = MIX_WIDTH - X_WIDTH
LRU_WIDTH = TM_WIDTH
LRU_BLOCKS = 4
LRU_BLOCK = LRU_WIDTH // LRU_BLOCKS
CONV_WIDTH = 4
LRU_C = 8.0
LRU_IN = 2 * LRU_WIDTH + X_WIDTH
DSA_HEADS = TM_WIDTH // HEAD_DIM
DSA_V_DIM = 128
IDX_HEADS = 4
IDX_DIM = 64
TOPK_MAX = 256
Q_BLOCK = 128
DSA_SIZES = (DSA_HEADS * HEAD_DIM, HEAD_DIM, DSA_V_DIM, IDX_HEADS * IDX_DIM, IDX_DIM, IDX_HEADS, X_WIDTH)
DSA_IN = int(sum(DSA_SIZES))
DSA_SPLITS = tuple(int(c) for c in np.cumsum(DSA_SIZES)[:-1])
REL_BUCKETS = 32
REL_MAX_DIST = 128
N_GROUPS = 4
EXPERTS_PER_GROUP = 8
N_EXPERTS = N_GROUPS * EXPERTS_PER_GROUP
TOP_K_IN_GROUP = 2
D_EXPERT = 512
MOE_BLOCK = 128
N_LRU_LAYERS = (DEPTH + 1) // 2
N_DSA_LAYERS = DEPTH // 2

kernel_name = "hybrid_rglru_dsa_memxattn_hmoe"

def rms_norm(x, g):
    xf = x.astype(jnp.float32)
    y = xf * lax.rsqrt(jnp.mean(xf * xf, axis=-1, keepdims=True) + EPS)
    return (y * g.astype(jnp.float32)).astype(x.dtype)

def rms_unit(x):
    xf = x.astype(jnp.float32)
    return (xf * lax.rsqrt(jnp.mean(xf * xf, axis=-1, keepdims=True) + EPS)).astype(x.dtype)

def t5_bucket(dist):
    max_exact = REL_BUCKETS // 2
    d = jnp.maximum(dist, 0)
    df = jnp.maximum(d, 1).astype(jnp.float32)
    large = max_exact + (jnp.log(df / max_exact) / math.log(REL_MAX_DIST / max_exact)
                         * (REL_BUCKETS - max_exact)).astype(jnp.int32)
    large = jnp.minimum(large, REL_BUCKETS - 1)
    return jnp.where(d < max_exact, d, large)

def memory_kv(mem, g, w):
    B, M, _ = mem.shape
    k, v = jnp.split(rms_norm(mem, g) @ w, 2, axis=-1)
    return k.reshape(B, M, X_HEADS, HEAD_DIM), v.reshape(B, M, X_HEADS, HEAD_DIM)

def memory_cross_attention(xq, mk, mv, gq, gk):
    B, S, _ = xq.shape
    q = rms_norm(xq.reshape(B, S, X_HEADS, HEAD_DIM), gq)
    k = rms_norm(mk, gk)
    logits = jnp.einsum('bshd,bmhd->bhsm', q, k).astype(jnp.float32) * HEAD_DIM ** -0.5
    p = jax.nn.softmax(logits, axis=-1).astype(mv.dtype)
    return jnp.einsum('bhsm,bmhd->bshd', p, mv).reshape(B, S, X_WIDTH)

def causal_depthwise_conv(x, w, b):
    S = x.shape[1]
    xp = jnp.pad(x, ((0, 0), (CONV_WIDTH - 1, 0), (0, 0)))
    out = b
    for k in range(CONV_WIDTH):
        out = out + xp[:, k:k + S] * w[k]
    return out

def rglru(x, w_a, b_a, w_x, b_x, lam):
    B, S, _ = x.shape
    xf = x.astype(jnp.float32)
    xb = xf.reshape(B, S, LRU_BLOCKS, LRU_BLOCK)
    r = jax.nn.sigmoid(jnp.einsum('bsni,nij->bsnj', xb, w_a.astype(jnp.float32)).reshape(B, S, LRU_WIDTH) + b_a)
    i = jax.nn.sigmoid(jnp.einsum('bsni,nij->bsnj', xb, w_x.astype(jnp.float32)).reshape(B, S, LRU_WIDTH) + b_x)
    log_a = -LRU_C * r * jax.nn.softplus(-lam.astype(jnp.float32))
    a = jnp.exp(log_a)
    u = jnp.sqrt(-jnp.expm1(2.0 * log_a)) * (i * xf)

    def combine(left, right):
        a1, b1 = left
        a2, b2 = right
        return a1 * a2, a2 * b1 + b2

    _, h = lax.associative_scan(combine, (a, u), axis=1)
    return h.astype(x.dtype)

def rglru_mixer(hn, mk, mv, w_in, conv_w, conv_b, w_a, b_a, w_x, b_x, lam, xq_g, xk_g):
    proj = hn @ w_in
    xs, gate, xq = jnp.split(proj, [LRU_WIDTH, 2 * LRU_WIDTH], axis=-1)
    xs = causal_depthwise_conv(xs, conv_w, conv_b)
    y = rglru(xs, w_a, b_a, w_x, b_x, lam) * jax.nn.gelu(gate)
    xo = memory_cross_attention(xq, mk, mv, xq_g, xk_g)
    return jnp.concatenate([y, xo], axis=-1)

def dsa_mixer(hn, mk, mv, w_in, q_g, k_g, w_uv, rel_bias, xq_g, xk_g):
    B, S, _ = hn.shape
    proj = hn @ w_in
    q, k, v, qi, ki, wi, xq = jnp.split(proj, DSA_SPLITS, axis=-1)
    q = rms_norm(q.reshape(B, S, DSA_HEADS, HEAD_DIM), q_g)
    k = rms_norm(k, k_g)
    qi = qi.reshape(B, S, IDX_HEADS, IDX_DIM)
    ki = rms_unit(ki)
    wi = wi * IDX_HEADS ** -0.5
    topk = min(TOPK_MAX, S // 4)
    n_blk = S // Q_BLOCK
    key_pos = jnp.arange(S, dtype=jnp.int32)

    def to_blocks(a):
        return jnp.swapaxes(a.reshape(B, n_blk, Q_BLOCK, *a.shape[2:]), 0, 1)

    def block_fn(args):
        qb, qib, wib, blk = args
        t = blk * Q_BLOCK + jnp.arange(Q_BLOCK, dtype=jnp.int32)
        dots = jnp.einsum('bqhd,bsd->bqhs', qib, ki).astype(jnp.float32) * IDX_DIM ** -0.5
        score = jnp.einsum('bqh,bqhs->bqs', wib.astype(jnp.float32), jax.nn.relu(dots))
        score = jnp.where((key_pos[None, :] <= t[:, None])[None], score, -jnp.inf)
        _, sel = lax.top_k(score, topk)
        k_sel = jax.vmap(lambda kk, ii: kk[ii])(k, sel)
        v_sel = jax.vmap(lambda vv, ii: vv[ii])(v, sel)
        dist = t[None, :, None] - sel
        bias = jnp.swapaxes(rel_bias[t5_bucket(dist)], -1, -2)
        logits = jnp.einsum('bqhd,bqkd->bqhk', qb, k_sel).astype(jnp.float32) * HEAD_DIM ** -0.5
        logits = logits + bias.astype(jnp.float32)
        logits = jnp.where((dist >= 0)[:, :, None, :], logits, -jnp.inf)
        p = jax.nn.softmax(logits, axis=-1).astype(v.dtype)
        o = jnp.einsum('bqhk,bqkc->bqhc', p, v_sel)
        return jnp.einsum('bqhc,hcd->bqhd', o, w_uv).reshape(B, Q_BLOCK, DSA_HEADS * HEAD_DIM)

    out = lax.map(block_fn, (to_blocks(q), to_blocks(qi), to_blocks(wi), jnp.arange(n_blk, dtype=jnp.int32)))
    y = jnp.swapaxes(out, 0, 1).reshape(B, S, DSA_HEADS * HEAD_DIM)
    xo = memory_cross_attention(xq, mk, mv, xq_g, xk_g)
    return jnp.concatenate([y, xo], axis=-1)

def grouped_swiglu(xt, eid, w_gate, w_up, w_down):
    N, D = xt.shape
    A = eid.shape[0]
    counts = jnp.bincount(eid, length=N_EXPERTS)
    padded = (counts + MOE_BLOCK - 1) // MOE_BLOCK * MOE_BLOCK
    seg_end = jnp.cumsum(padded)
    pad_start = seg_end - padded
    start = jnp.cumsum(counts) - counts
    order = jnp.argsort(eid)
    eid_sorted = eid[order]
    dest_sorted = (pad_start[eid_sorted] + jnp.arange(A) - start[eid_sorted]).astype(jnp.int32)
    dest = jnp.zeros((A,), jnp.int32).at[order].set(dest_sorted)
    n_blocks = -(-A // MOE_BLOCK) + N_EXPERTS
    P = n_blocks * MOE_BLOCK
    tok = jnp.arange(A, dtype=jnp.int32) // TOP_K_IN_GROUP
    buf = jnp.zeros((P, D), xt.dtype).at[dest].set(xt[tok])
    block_eid = jnp.minimum(jnp.searchsorted(seg_end, jnp.arange(n_blocks) * MOE_BLOCK, side='right'),
                            N_EXPERTS - 1)

    def expert_block(args):
        xb, e = args
        return (jax.nn.silu(xb @ w_gate[e]) * (xb @ w_up[e])) @ w_down[e]

    out = lax.map(expert_block, (buf.reshape(n_blocks, MOE_BLOCK, D), block_eid))
    return out.reshape(P, D)[dest]

def hier_moe(h, w_grp, b_grp, w_rt, b_rt, w_gate, w_up, w_down):
    B, S, D = h.shape
    xt = h.reshape(B * S, D)
    N = xt.shape[0]
    p_grp = jax.nn.softmax((xt @ w_grp).astype(jnp.float32) + b_grp, axis=-1)
    p_g, g_sel = lax.top_k(p_grp, 1)
    e_logits = ((xt @ w_rt).astype(jnp.float32) + b_rt).reshape(N, N_GROUPS, EXPERTS_PER_GROUP)
    e_logits = jnp.take_along_axis(e_logits, g_sel[:, :, None], axis=1)[:, 0]
    p_e = jax.nn.softmax(e_logits, axis=-1)
    v2, e_sel = lax.top_k(p_e, TOP_K_IN_GROUP)
    gate = p_g * v2 / jnp.sum(v2, axis=-1, keepdims=True)
    eid = (g_sel * EXPERTS_PER_GROUP + e_sel).reshape(-1).astype(jnp.int32)
    y = grouped_swiglu(xt, eid, w_gate, w_up, w_down).reshape(N, TOP_K_IN_GROUP, D)
    out = jnp.sum(y * gate[..., None].astype(y.dtype), axis=1)
    return out.reshape(B, S, D)

def setup_inputs(seed: int = 0) -> dict:
    key = jax.random.key(seed)
    ks = iter(jax.random.split(key, 40))
    f32 = jnp.float32

    def nrm(shape, scale):
        return jax.random.normal(next(ks), shape, f32) * scale

    def gain(shape):
        return 1.0 + nrm(shape, 0.02)

    NL, ND = N_LRU_LAYERS, N_DSA_LAYERS
    x = nrm((BATCH, SEQ, D_MODEL), 1.0)
    mem = nrm((BATCH, N_MEM, D_MODEL), 1.0)
    norm_mix = gain((DEPTH, D_MODEL))
    norm_ffn = gain((DEPTH, D_MODEL))
    mem_norm = gain((DEPTH, D_MODEL))
    w_mem_kv = nrm((DEPTH, D_MODEL, 2 * X_WIDTH), D_MODEL ** -0.5)
    xq_norm = gain((DEPTH, HEAD_DIM))
    xk_norm = gain((DEPTH, HEAD_DIM))
    w_out = nrm((DEPTH, MIX_WIDTH, D_MODEL), MIX_WIDTH ** -0.5)
    lru_w_in = nrm((NL, D_MODEL, LRU_IN), D_MODEL ** -0.5)
    lru_conv_w = nrm((NL, CONV_WIDTH, LRU_WIDTH), CONV_WIDTH ** -0.5)
    lru_conv_b = nrm((NL, LRU_WIDTH), 0.01)
    lru_w_a = nrm((NL, LRU_BLOCKS, LRU_BLOCK, LRU_BLOCK), LRU_BLOCK ** -0.5)
    lru_b_a = nrm((NL, LRU_WIDTH), 0.01)
    lru_w_x = nrm((NL, LRU_BLOCKS, LRU_BLOCK, LRU_BLOCK), LRU_BLOCK ** -0.5)
    lru_b_x = nrm((NL, LRU_WIDTH), 0.01)
    a0 = jax.random.uniform(next(ks), (NL, LRU_WIDTH), f32, 0.9, 0.999)
    p = a0 ** (1.0 / LRU_C)
    lru_lambda = jnp.log(p) - jnp.log1p(-p)
    dsa_w_in = nrm((ND, D_MODEL, DSA_IN), D_MODEL ** -0.5)
    dsa_q_norm = gain((ND, HEAD_DIM))
    dsa_k_norm = gain((ND, HEAD_DIM))
    dsa_w_uv = nrm((ND, DSA_HEADS, DSA_V_DIM, HEAD_DIM), DSA_V_DIM ** -0.5)
    rel_bias = nrm((REL_BUCKETS, DSA_HEADS), 0.5)
    moe_w_group = nrm((DEPTH, D_MODEL, N_GROUPS), D_MODEL ** -0.5)
    moe_b_group = nrm((DEPTH, N_GROUPS), 0.01)
    moe_w_router = nrm((DEPTH, D_MODEL, N_EXPERTS), D_MODEL ** -0.5)
    moe_b_router = nrm((DEPTH, N_EXPERTS), 0.01)
    moe_w_gate = nrm((DEPTH, N_EXPERTS, D_MODEL, D_EXPERT), D_MODEL ** -0.5)
    moe_w_up = nrm((DEPTH, N_EXPERTS, D_MODEL, D_EXPERT), D_MODEL ** -0.5)
    moe_w_down = nrm((DEPTH, N_EXPERTS, D_EXPERT, D_MODEL), D_EXPERT ** -0.5)
    return {"x": x, "mem": mem, "norm_mix": norm_mix, "norm_ffn": norm_ffn, "mem_norm": mem_norm,
            "w_mem_kv": w_mem_kv, "xq_norm": xq_norm, "xk_norm": xk_norm, "w_out": w_out,
            "lru_w_in": lru_w_in, "lru_conv_w": lru_conv_w, "lru_conv_b": lru_conv_b,
            "lru_w_a": lru_w_a, "lru_b_a": lru_b_a, "lru_w_x": lru_w_x, "lru_b_x": lru_b_x,
            "lru_lambda": lru_lambda, "dsa_w_in": dsa_w_in, "dsa_q_norm": dsa_q_norm,
            "dsa_k_norm": dsa_k_norm, "dsa_w_uv": dsa_w_uv, "rel_bias": rel_bias,
            "moe_w_group": moe_w_group, "moe_b_group": moe_b_group, "moe_w_router": moe_w_router,
            "moe_b_router": moe_b_router, "moe_w_gate": moe_w_gate, "moe_w_up": moe_w_up,
            "moe_w_down": moe_w_down}

def reference(x, mem, norm_mix, norm_ffn, mem_norm, w_mem_kv, xq_norm, xk_norm, w_out,
              lru_w_in, lru_conv_w, lru_conv_b, lru_w_a, lru_b_a, lru_w_x, lru_b_x, lru_lambda,
              dsa_w_in, dsa_q_norm, dsa_k_norm, dsa_w_uv, rel_bias,
              moe_w_group, moe_b_group, moe_w_router, moe_b_router, moe_w_gate, moe_w_up, moe_w_down):
    for i in range(DEPTH):
        j = i // 2
        mk, mv = memory_kv(mem, mem_norm[i], w_mem_kv[i])
        hn = rms_norm(x, norm_mix[i])
        if i % 2 == 0:
            mixed = rglru_mixer(hn, mk, mv, lru_w_in[j], lru_conv_w[j], lru_conv_b[j], lru_w_a[j],
                                lru_b_a[j], lru_w_x[j], lru_b_x[j], lru_lambda[j], xq_norm[i], xk_norm[i])
        else:
            mixed = dsa_mixer(hn, mk, mv, dsa_w_in[j], dsa_q_norm[j], dsa_k_norm[j], dsa_w_uv[j],
                              rel_bias, xq_norm[i], xk_norm[i])
        x = x + mixed @ w_out[i]
        x = x + hier_moe(rms_norm(x, norm_ffn[i]), moe_w_group[i], moe_b_group[i], moe_w_router[i],
                         moe_b_router[i], moe_w_gate[i], moe_w_up[i], moe_w_down[i])
    return x


_drawn_inputs = setup_inputs


def setup_inputs(seed=0):
    import zlib

    import numpy as np

    out = dict(_drawn_inputs(seed))
    spreads = {}
    factors = {'mem_norm': 2.895,
     'xq_norm': 4.043,
     'xk_norm': 2.985,
     'lru_b_a': 8.0,
     'lru_b_x': 4.479,
     'dsa_q_norm': 5.574,
     'dsa_k_norm': 4.362,
     'moe_b_router': 2.721}
    for name, (base, spread) in spreads.items():
        noise = np.random.default_rng([zlib.crc32(name.encode()), seed]).standard_normal(out[name].shape)
        drawn = base * np.exp(spread * noise) if base else spread * noise
        out[name] = __import__('jax').numpy.asarray(drawn.astype(out[name].dtype))
    for name, factor in factors.items():
        out[name] = (out[name] * factor).astype(out[name].dtype)
    return out
```

```python
from contextlib import ExitStack

import numpy as np

import concourse.bass as bass
from concourse import mybir

F32 = mybir.dt.float32
BF16 = mybir.dt.bfloat16
I32 = mybir.dt.int32
U32 = mybir.dt.uint32
ALU = mybir.AluOpType
ACT = mybir.ActivationFunctionType
AX = mybir.AxisListType

P = 128
D = 1024
KD = D // P
S = 512
NT = S // P
M = 256
EPS = 1e-6
XH, HD = 4, 64
XW = XH * HD
LRU = D - XW
NC = LRU // P
LB = LRU // 4
CONV = 4
HEADS = LRU // HD
VD = 128
TOPK = min(256, S // 4)
W0 = 2 * LRU + XW
IH = 4
C_Q, C_K, C_V = 0, LRU, LRU + HD
C_QI = C_V + VD
C_KI = C_QI + IH * HD
C_WI = C_KI + HD
C_XQ = C_WI + IH
W1 = C_XQ + XW
NB, MAXD = 32, 128
NG, EG = 4, 8
NE = NG * EG
FE = 512
KF = FE // P
CAP = 64
NBLK = S // CAP
OVMAX = 2 * S // CAP
NS = 3
R = NG + NE
BIG = -1.0e30
TAKEN = -3.0e38
NOTOK = 4096.0

R_CW, R_CB, R_BA, R_BX, R_LAM = 0, CONV * NC, (CONV + 1) * NC, (CONV + 2) * NC, (CONV + 3) * NC
R_XQ = (CONV + 4) * NC
NPRM = R_XQ + 6


def bucket_onehot():
    d = S - 1 - np.arange(S + P, dtype=np.int64)
    d = np.maximum(d, 0)
    df = np.maximum(d, 1).astype(np.float32)
    half = NB // 2
    large = half + (np.log(df / np.float32(half)) / np.float32(np.log(MAXD / half)) * np.float32(NB - half)).astype(np.int32)
    b = np.where(d < half, d, np.minimum(large, NB - 1))
    return (np.arange(NB)[:, None] == b[None, :]).astype(np.float32)


class Jobs:

    def __init__(self):
        self.number, self.reader, self.before = {}, [], []
        self.count = {"act": 0, "dve": 0}

    def add(self, name, reader):
        self.number[name] = len(self.reader)
        self.reader.append(reader)
        self.count[reader] += 1
        self.before.append(dict(self.count))

    def emptied(self, name):
        n = self.number[name]
        return self.reader[n], self.before[n][self.reader[n]]


def lru_order():
    steps = [("conv", c) for c in range(3)]
    for c in range(NC):
        steps += [("rec", c), ("conv", c + 3) if c < 3 else ("gate", c - 3)]
    return steps + [("gate", c) for c in range(NC - 3, NC)]


def attention_groups():
    return [(qb, g) for qb in range(NT) for g in range(HEADS // 4)]


def pt_reader(qb, g, s):
    return "act" if (s + g) % 2 else "dve"


def plan():
    j = Jobs()
    for L in range(2):
        for mt in range(2):
            for h in range(2):
                j.add(f"{L}.memT.{mt}.{h}", "dve")
        for c in range(2):
            j.add(f"{L}.memK.{c}", "act")
        for mt in range(2):
            j.add(f"{L}.memV.{mt}", "act")
        if L == 0:
            for name in ("params", "bias0", "bias1"):
                j.add(name, "act")
        for t in range(NT):
            for h in range(2):
                j.add(f"{L}.xT.{t}.{h}", "dve")
        if L == 0:
            j.add("0.sq.memK", "act")
            for what, c in lru_order():
                if what == "rec":
                    j.add(f"0.ra.{c}", "act")
                    j.add(f"0.rx.{c}", "act")
                elif what == "gate":
                    j.add(f"0.gate.{c}", "act")
                else:
                    j.add(f"0.xs.{c}", "act")
                    if c == 2:
                        for name in ("xq.0", "xq.1", "sq.xq.0", "sq.xq.1"):
                            j.add(f"0.{name}", "act")
        else:
            j.add("1.sq.memK", "act")
            j.add("1.ki", "act")
            j.add("1.qi.0", "act")
            j.add("1.sq.ki", "act")
            j.add("1.qi.1", "act")
            j.add("1.v", "act")
            j.add("1.wi", "act")
            for qb in range(1, NT):
                for h in range(IH):
                    j.add(f"1.dot.{qb}.{h}", "act")
            last = None
            for name in ["k"] + [f"q.{c}" for c in range(NC)] + ["xq.0", "xq.1"]:
                j.add(f"1.{name}", "act")
                if last:
                    j.add(f"1.sq.{last}", "act")
                last = name
            j.add(f"1.sq.{last}", "act")
        for t in range(NT + 1):
            if t < NT:
                for par in range(2):
                    j.add(f"{L}.xl.{t}.{par}", "act")
            if t:
                j.add(f"{L}.xp.{t - 1}.0", "act")
                j.add(f"{L}.xp.{t - 1}.1", "dve")
                j.add(f"{L}.xo.{t - 1}", "dve")
        if L == 1:
            gs = attention_groups()
            for n in range(len(gs) + 1):
                if n < len(gs):
                    qb, g = gs[n]
                    for h in range(4):
                        j.add(f"1.l.{qb}.{g}.{h}", "dve")
                if n:
                    qb, g = gs[n - 1]
                    for s in range(qb + 1):
                        j.add(f"1.pt.{qb}.{g}.{s}", pt_reader(qb, g, s))
                    j.add(f"1.pv.{qb}.{g}", "act")
                    j.add(f"1.uv.{qb}.{g}", "dve")
        for t in range(NT):
            for h in range(2):
                j.add(f"{L}.out.{t}.{h}", "dve")
        for t in range(NT):
            for h in range(2):
                j.add(f"{L}.fT.{t}.{h}", "dve")
        j.add(f"{L}.route", "dve")
        j.add(f"{L}.rank", "dve")
    return j


def hybrid_trunk(nc, a, out):
    jobs = plan()
    scratch_bias = nc.dram_tensor("scratch_bias", (HEADS, S + P), F32).ap()
    scratch_rep = nc.dram_tensor("scratch_rep", (P, HEADS, S + P), F32).ap()
    scratch_xn = [nc.dram_tensor(f"scratch_xn{L}", (S, D), F32).ap() for L in range(2)]
    scratch_tab = [nc.dram_tensor(f"scratch_tab{L}", (S * NE, 2), F32).ap() for L in range(2)]
    scratch_ov = nc.dram_tensor("scratch_ov", (2, OVMAX, 2), I32)
    onehot_dram = nc.inline_tensor(bucket_onehot(), name="bucket_onehot")

    with ExitStack() as ctx:
        def sb(name, shape, dt=F32):
            return ctx.enter_context(nc.sbuf_tensor(name, shape, dt))

        def sem(name):
            return ctx.enter_context(nc.semaphore(name))

        SLOT = 3 * KD * FE
        arena = sb("arena", [P, NS * SLOT])
        x = sb("x", [P, NT, D])
        xT = sb("xT", [P, KD, S])
        mix = sb("mix", [P, 8, S])
        xn = mix[:, :, :].rearrange("p a b -> p (a b)").rearrange("p (t d) -> p t d", t=NT)
        ident = sb("ident", [P, P])
        identb = sb("identb", [P, P], BF16)
        ones_head = sb("ones_head", [P, P])
        before = sb("before", [P, P], BF16)
        ones_b = sb("ones_b", [P, P], BF16)
        iota_tok = sb("iota_tok", [P, S])
        iota_e = sb("iota_e", [P, NE])
        thr = sb("thr", [P, NBLK - 1, NE])
        code_e = sb("code_e", [P, NBLK - 1, NE])
        code_r = sb("code_r", [P, NBLK - 1, NE])
        rank_w = sb("rank_w", [P, NG])
        tokid = sb("tokid", [P, NT])
        place1 = sb("place1", [P, 1])
        prm_rows = sb("prm_rows", [NPRM, P])
        prm = sb("prm", [P, NPRM])
        eps = sb("eps", [P, 1])
        gains = sb("gains", [P, 6, KD])
        w_route = sb("w_route", [P, KD, R])
        b_route = sb("b_route", [P, 2, R])
        memKT = sb("memKT", [P, 2, M])
        memV = sb("memV", [P, 2, XW])
        small = sb("small", [P, 256])
        v8 = sb("v8", [P, NT, 8])
        i8 = sb("i8", [P, NT, 8], U32)
        choice = sb("choice", [P, NT, NE], BF16)
        dest = sb("dest", [P, 2, NT], I32)
        pay = sb("pay", [P, 2, NT, 2])
        tabS = sb("tabS", [P, NE + 1, 2])
        cur = sb("cur", [P, 2])
        idx = sb("idx", [CAP, NS], I32)
        ov_code = sb("ov_code", [P, 2], I32)
        ov_list = sb("ov_list", [1, 2 * OVMAX], I32)
        ov_n = sb("ov_n", [1, 1], I32)
        ov_cur = sb("ov_cur", [P, 2])
        ov_idx = sb("ov_idx", [CAP, 1], I32)
        ps = ctx.enter_context(nc.psum_tensor("ps", [P, 8, 512], F32))

        def area(at, *shape, dt=F32):
            n = int(np.prod(shape))
            words = n if dt == F32 else n // 2
            v = arena[:, at:at + words]
            if dt != F32:
                v = v.bitcast(dt)
            if len(shape) == 1:
                return v
            names = "abcd"[:len(shape)]
            return v.rearrange(f"p ({' '.join(names)}) -> p {' '.join(names)}", **dict(zip(names[1:], shape[1:])))

        w_out = area(NS * SLOT - KD * D, KD, D)
        start_area = area(NS * SLOT - KD * D, KD * D)
        w_in = [area(NS * SLOT - KD * D - KD * W0, KD, W0), area(NS * SLOT - KD * D - KD * W1, KD, W1)]
        lo1 = NS * SLOT - KD * D - KD * W1
        lo0 = NS * SLOT - KD * D - KD * W0
        w_kv = area(0, KD, 2 * XW)
        mem = area(4096, 2, D)
        memT = area(6144, KD, M)
        bucket_oh = start_area[0:NB, 0:S + P]
        bucket_bias = start_area[0:NB, 640:640 + HEADS]
        bias_rows = start_area[0:HEADS, 1024:1024 + S + P]
        xs = area(8192, NC, S + CONV - 1)
        gate_w = area(11284, 2, 2, 3, LB)
        xc = area(0, NC, S)
        xqT = [area(3072, 2, S), area(5120, 2, S)]
        lru = area(4096, 2, 3, S)
        sqb = [area(7168, 2, S), area(6144, 2, S)]
        rsb = [area(4096, 2, S), area(7168, 2, S)]
        qT = area(0, NC, S)
        qiT = area(3072, 2, S)
        kT = area(4096, S)
        kiT = area(4608, S)
        T_all = area(8192, HEADS, S)
        v_sb = area(14336, NT, VD)
        w_uv = area(14848, HEADS, HD)
        wi_sb = area(15616, NT, IH)
        att = [lo0, lo1]
        P_sb = [area(att[L], 2, 4, 512) for L in range(2)]
        PT_sb = [area(att[L] + 4096, 2, 4, 512) for L in range(2)]
        oT = area(att[1] + 8192, 2, 512)
        masks = [area(15680 + 32 * q * (q + 1), (q + 1) * P, dt=BF16) for q in range(NT)]
        relu = mix[:, 0:3, :]
        score = [None] + [mix[:, 2 + q, :] for q in range(1, NT)]
        xn_ffn = area(2 * SLOT, NT, D)
        slots = []
        for s in range(NS):
            slots.append((area(s * SLOT, KD, FE), area(s * SLOT + KD * FE, KD, FE), area(s * SLOT + 2 * KD * FE, KF, D)))
        flatT = xT[:, :, :].rearrange("p a b -> p (a b)")
        tokT = flatT[:, 0:512].rearrange("p (k n) -> p k n", k=KD)
        onehot = flatT[:, 512:768].bitcast(BF16)
        y_hm = [flatT[:, 768 + 256 * h:1024 + 256 * h].bitcast(BF16) for h in range(2)]
        y_lo = flatT[:, 1280:1536].bitcast(BF16)
        silu = flatT[:, 1536:2048]
        h_sb = flatT[:, 2048:2560]
        hT = flatT[:, 2560:2816].rearrange("p (j n) -> p j n", j=KF)
        flatM = mix[:, :, :].rearrange("p a b -> p (a b)")
        xg = [flatM[0:CAP, s * D:(s + 1) * D] for s in range(NS)]
        y_rest = flatM[:, NS * D:NS * D + 512]
        HALF = [slice(0, CAP), slice(CAP, P)]
        route_area = flatT[:, 2816:4096]

        ld = {n: sem(f"ld_{n}") for n in ["mem", "x", "prm", "onehot", "gains", "broute", "wkv", "win", "winq", "wing", "wg",
                                          "wout", "wr", "bias", "wuv", "tab", "ovl"]}
        filled = sem("filled")
        emptied = {"act": sem("emptied_act"), "dve": sem("emptied_dve")}
        consts = sem("consts")
        act_line, dve_line, pool_line = sem("act_line"), sem("dve_line"), sem("pool_line")
        row_sums = sem("row_sums")
        rows_normed = sem("rows_normed")
        sq_ready = sem("sq_ready")
        feat_normed = sem("feat_normed")
        gain_ready = sem("gain_ready")
        xc_ready = sem("xc_ready")
        lru_tanh = sem("lru_tanh")
        lru_log = sem("lru_log")
        lru_exp = sem("lru_exp")
        lru_sq = sem("lru_sq")
        lru_var = sem("lru_var")
        lru_h = sem("lru_h")
        lru_root = sem("lru_root")
        lru_y = sem("lru_y")
        lru_par_a, lru_par_d = sem("lru_par_a"), sem("lru_par_d")
        dots_used = sem("dots_used")
        causal = sem("causal")
        masked = sem("masked")
        x_max = sem("x_max")
        x_inv = sem("x_inv")
        x_prob = sem("x_prob")
        l_max = sem("l_max")
        l_exp = sem("l_exp")
        l_inv = sem("l_inv")
        l_prob = sem("l_prob")
        r_diff, r_exp = sem("r_diff"), sem("r_exp")
        chosen = sem("chosen")
        routed = sem("routed")
        xn_stored = sem("xn_stored")
        tab_zero = sem("tab_zero")
        scattered = sem("scattered")
        tab_loaded = sem("tab_loaded")
        ov_stored = sem("ov_stored")
        bias_stored, bias_spread = sem("bias_stored"), sem("bias_spread")
        gu_landed = [sem(f"gu_landed{s}") for s in range(NS)]
        d_landed = [sem(f"d_landed{s}") for s in range(NS)]
        gathered = [sem(f"gathered{s}") for s in range(NS)]
        idx_ready, cur_ready = sem("idx_ready"), sem("cur_ready")
        names = ["xt_psum", "xt_sbuf", "gu_psum", "silu_done", "h_done", "ht_psum", "ht_sbuf", "y_psum", "y_high", "y_rest",
                 "y_mid", "y_low",
                 "g_done", "c_psum", "c_added"]
        m = {n: sem(n) for n in names}
        ov = [{n: sem(f"ov{L}_{n}") for n in names + ["landed", "cur", "idx", "gathered"]} for L in range(2)]
        moe_done = sem("moe_done")
        stored = sem("stored")

        def wait_alone(eng, s, value):
            eng.wait_ge(s, value)
            eng.nop(nofuse=True)

        def wait_filled(eng, name):
            eng.wait_ge(filled, jobs.number[name] + 1)

        def wait_emptied(eng, name):
            who, n = jobs.emptied(name)
            eng.wait_ge(emptied[who], n)

        def bank(name):
            return ps[:, jobs.number[name] % 8, :]

        class Line:

            def __init__(self, eng, s):
                self.eng, self.s, self.n = eng, s, 0

            def step(self, ins):
                ins.then_inc(self.s, 1)
                self.n += 1

            def settle(self):
                self.eng.wait_ge(self.s, self.n)

            def link(self, ins):
                self.step(ins)
                self.settle()

        rows = {}
        for L in range(2):
            for kind, n in (("mem", 2), ("mix", NT), ("ffn", NT)):
                for t in range(n):
                    rows[L, kind, t] = len(rows) + 1
        feats = {}
        for f in ["0.memK", "0.xq.0", "0.xq.1", "1.memK", "1.ki", "1.k"] + [f"1.q.{c}" for c in range(NC)] + ["1.xq.0", "1.xq.1"]:
            feats[f] = len(feats) + 1

        def rs_view(key):
            return rsb[int(key[0])][:, feats[key] % 2, :]

        slot_base = [[0, 0, 0], [11, 11, 10]]

        block = ctx.enter_context(nc.Block())

        @block.sync
        def _(sp):
            def expert_weights(L, e, s, before_):
                wg, wu, wd = slots[s]
                if before_ is not None:
                    sp.wait_ge(m["gu_psum"], before_)
                sp.dma_start(wg, a["moe_w_gate"][L, bass.ds(e, 1)].rearrange("a (p k) n -> p (a k) n", k=KD)).then_inc(gu_landed[s], 16)
                sp.dma_start(wu, a["moe_w_up"][L, bass.ds(e, 1)].rearrange("a (p k) n -> p (a k) n", k=KD)).then_inc(gu_landed[s], 16)
                if before_ is not None:
                    sp.wait_ge(m["y_psum"], before_)
                sp.dma_start(wd, a["moe_w_down"][L, bass.ds(e, 1)].rearrange("a (p j) n -> p (a j) n", j=KF)).then_inc(d_landed[s], 16)

            for L in range(2):
                if L:
                    sp.wait_ge(moe_done, L)
                sp.dma_start(mem, a["mem"][0].rearrange("(t p) d -> p t d", p=P)).then_inc(ld["mem"], 16)
                sp.dma_start(w_kv, a["w_mem_kv"][L].rearrange("(p k) n -> p k n", k=KD)).then_inc(ld["wkv"], 16)
                w = a["lru_w_in"][0] if L == 0 else a["dsa_w_in"][0]
                w = w.rearrange("(p k) n -> p k n", k=KD)
                if L == 0:
                    sp.dma_start(x[:], a["x"][0].rearrange("(t p) d -> p t d", p=P)).then_inc(ld["x"], 16)
                    sp.wait_ge(ld["broute"], 32)
                    for n, c0, c1 in (("win", 0, LRU), ("winq", 2 * LRU, W0), ("wing", LRU, 2 * LRU)):
                        sp.dma_start(w_in[0][:, :, c0:c1], w[:, :, c0:c1]).then_inc(ld[n], 16)
                else:
                    sp.dma_start(w_in[1], w).then_inc(ld["win"], 16)
                if L == 0:
                    for g, src in enumerate((a["lru_w_a"][0], a["lru_w_x"][0])):
                        for pair in range(2):
                            even, odd = src[2 * pair], src[2 * pair + 1]
                            sp.dma_start(gate_w[:, g, pair, 0, :], even[0:128, :]).then_inc(ld["wg"], 16)
                            sp.dma_start(gate_w[0:64, g, pair, 1, :], even[128:LB, :]).then_inc(ld["wg"], 16)
                            sp.dma_start(gate_w[64:128, g, pair, 1, :], odd[0:64, :]).then_inc(ld["wg"], 16)
                            sp.dma_start(gate_w[:, g, pair, 2, :], odd[64:LB, :]).then_inc(ld["wg"], 16)
                else:
                    sp.wait_ge(bias_spread, 16)
                    toeplitz = bass.AP(scratch_rep.tensor, P - 1, [[HEADS * (S + P) - 1, P], [S + P, HEADS], [1, S]])
                    sp.dma_start(T_all, toeplitz).then_inc(ld["bias"], 16)
                    sp.dma_start(w_uv, a["dsa_w_uv"][0].rearrange("h c d -> c h d")).then_inc(ld["wuv"], 16)
                if L == 0:
                    sp.wait_ge(tab_zero, 32)
                    sp.wait_ge(bias_stored, 16)
                sp.dma_start(w_out, a["w_out"][L].rearrange("(c p) n -> p c n", p=P)).then_inc(ld["wout"], 16)
                if L:
                    wait_filled(sp, "0.route")
                sp.dma_start(w_route[:, :, 0:NG], a["moe_w_group"][L].rearrange("(p k) n -> p k n", k=KD)).then_inc(ld["wr"], 16)
                sp.dma_start(w_route[:, :, NG:R], a["moe_w_router"][L].rearrange("(p k) n -> p k n", k=KD)).then_inc(ld["wr"], 16)
                if L == 0:
                    sp.wait_ge(bias_stored, 16)
                    sp.dma_start(scratch_rep, scratch_bias.unsqueeze(0).to_broadcast([P, HEADS, S + P])).then_inc(bias_spread, 16)
                wait_filled(sp, f"{L}.out.0.0")
                expert_weights(L, 0, 0, None)
                expert_weights(L, 1, 1, None)
                for t in range(NT):
                    sp.wait_ge(rows_normed, rows[L, "ffn", t])
                    sp.dma_start(scratch_xn[L][t * P:(t + 1) * P, :], xn_ffn[:, t, :]).then_inc(xn_stored, 16)
                sp.wait_ge(xn_stored, 16 * NT * (L + 1))
                wait_filled(sp, f"{L}.fT.{NT - 1}.1")
                expert_weights(L, 2, 2, None)
                sp.wait_ge(scattered, 16 * 2 * NT * (L + 1))
                tab = scratch_tab[L].rearrange("(s e) c -> s e c", e=NE)
                for h in range(2):
                    sp.dma_start(tabS[h * CAP:(h + 1) * CAP, 0:NE, :], tab[0:CAP]).then_inc(tab_loaded, 16)
                sp.wait_ge(chosen, 2 * L + 2)
                sp.dma_start(scratch_ov.ap()[L], ov_code[0:OVMAX, :]).then_inc(ov_stored, 16)
                with sp.Fori(0, (NE - 5) // 3) as i:
                    for j in range(3):
                        expert_weights(L, i * 3 + (3 + j), j, i * 3 + (NE * L + 1 + j))
                for e in (NE - 2, NE - 1):
                    expert_weights(L, e, e % NS, NE * L + e - 2)
                sp.wait_ge(ov_stored, 16 * (L + 1))
                sp.dma_start(ov_list[:], scratch_ov.ap()[L:L + 1].rearrange("a n c -> a (n c)")).then_inc(ld["ovl"], 16)
                o = ov[L]
                sp.wait_ge(ld["ovl"], 16 * (L + 1))
                n_ov = sp.value_load(ov_n[0:1, 0:1], min_val=0, max_val=OVMAX)
                with sp.If(n_ov > 0):
                    sp.wait_ge(m["y_psum"], NE * (L + 1))
                    with sp.Fori(0, n_ov) as i:
                        e = sp.value_load(ov_list[0:1, bass.ds(i * 2, 1)], min_val=0, max_val=NE - 1)
                        r = sp.value_load(ov_list[0:1, bass.ds(i * 2 + 1, 1)], min_val=0, max_val=(NBLK - 1) * CAP * NE + NE - 1)
                        wg, wu, wd = slots[0]
                        sp.dma_start(wg, a["moe_w_gate"][L, bass.ds(e, 1)].rearrange("a (p k) n -> p (a k) n", k=KD)).then_inc(o["landed"], 16)
                        sp.dma_start(wu, a["moe_w_up"][L, bass.ds(e, 1)].rearrange("a (p k) n -> p (a k) n", k=KD)).then_inc(o["landed"], 16)
                        sp.dma_start(wd, a["moe_w_down"][L, bass.ds(e, 1)].rearrange("a (p j) n -> p (a j) n", j=KF)).then_inc(o["landed"], 16)
                        for h in range(2):
                            sp.dma_start(ov_cur[h * CAP:(h + 1) * CAP, :],
                                         scratch_tab[L][bass.ds(r, CAP, NE), :]).then_inc(o["cur"], 16)
                        wait_alone(sp, o["g_done"], i + 1)
                        wait_alone(sp, o["idx"], i + 1)
                        wait_alone(sp, o["y_psum"], i + 1)
            sp.wait_ge(moe_done, 2)
            for t in range(NT):
                sp.dma_start(out[0, t * P:(t + 1) * P, :], x[:, t, :]).then_inc(stored, 16)
            sp.wait_ge(stored, 16 * NT)

        @block.gpsimd
        def _(pool):
            line = Line(pool, pool_line)
            for t_, val in ((ident, 0.0), (identb, 0.0), (before, 0.0), (ones_b, 1.0), (ones_head, 0.0)):
                line.step(pool.memset(t_[:], val))
            line.step(pool.memset(eps[:], EPS))
            line.step(pool.memset(tabS[:, NE, 0:1], NOTOK))
            line.step(pool.memset(tabS[:, NE, 1:2], 0.0))
            line.settle()
            for t_ in (ident, identb):
                line.step(pool.affine_select(out=t_[:], in_=t_[:], compare_op=ALU.not_equal, fill=1.0, base=0,
                                             pattern=[[-1, P]], channel_multiplier=1))
            line.step(pool.affine_select(out=before[:], in_=before[:], compare_op=ALU.is_ge, fill=1.0, base=0,
                                         pattern=[[-1, P]], channel_multiplier=1))
            for h in range(2):
                line.settle()
                line.link(pool.memset(ones_head[h * HD:(h + 1) * HD, h * HD:(h + 1) * HD], 1.0))
            line.step(pool.iota(iota_tok[:], pattern=[[1, S]], base=0, channel_multiplier=0, allow_small_or_imprecise_dtypes=True))
            line.step(pool.iota(iota_e[:], pattern=[[1, NE]], base=0, channel_multiplier=0, allow_small_or_imprecise_dtypes=True))
            line.step(pool.iota(thr[:], pattern=[[CAP, NBLK - 1], [0, NE]], base=CAP, channel_multiplier=0, allow_small_or_imprecise_dtypes=True))
            line.step(pool.iota(code_e[:], pattern=[[0, NBLK - 1], [1, NE]], base=0, channel_multiplier=0, allow_small_or_imprecise_dtypes=True))
            line.step(pool.iota(code_r[:], pattern=[[CAP * NE, NBLK - 1], [1, NE]], base=CAP * NE, channel_multiplier=0, allow_small_or_imprecise_dtypes=True))
            line.step(pool.iota(rank_w[:], pattern=[[-1, NG]], base=NG, channel_multiplier=0, allow_small_or_imprecise_dtypes=True))
            line.step(pool.iota(tokid[:], pattern=[[P, NT]], base=0, channel_multiplier=1, allow_small_or_imprecise_dtypes=True))
            line.step(pool.iota(place1[:], pattern=[[0, 1]], base=1, channel_multiplier=1, allow_small_or_imprecise_dtypes=True))
            empty = start_area[:, 2048:2048 + 2 * S * NE // P].rearrange("p (n c) -> p n c", c=2)
            line.step(pool.memset(empty[:, :, 0], NOTOK))
            line.step(pool.memset(empty[:, :, 1], 0.0))
            line.step(pool.memset(xs[:, :, 0:CONV - 1], 0.0))
            line.settle()
            pool.tensor_copy(pay[:, :, :, 0], tokid[:].unsqueeze(1).to_broadcast([P, 2, NT])).then_inc(consts, 1)
            for L in range(2):
                pool.dma_start(scratch_tab[L].rearrange("(p n) c -> p n c", p=P), empty).then_inc(tab_zero, 16)

            def scale_rows(buf, inv, n_heads, width):
                ins = None
                for h in range(n_heads):
                    ins = pool.tensor_scalar(buf[:, h, 0:width], buf[:, h, 0:width], inv[:, h:h + 1], 1.0, ALU.mult, ALU.mult)
                return ins

            def gather(L, e, s, n, first):
                if not first:
                    wait_alone(pool, m["xt_psum"], n - 2)
                pool.tensor_copy(idx[:, s:s + 1], tabS[0:CAP, e, 0:1] if isinstance(e, int) else
                                 tabS[0:CAP, bass.ds(e, 1), 0:1].rearrange("p a b -> p (a b)")).then_inc(idx_ready, 1)
                wait_alone(pool, idx_ready, n + 1)
                pool.indirect_dma_start(out=xg[s], out_offset=None, in_=scratch_xn[L],
                                        in_offset=bass.IndirectOffsetOnAxis(ap=idx[:, s:s + 1], axis=0),
                                        bounds_check=S - 1, oob_is_err=False).then_inc(gathered[s], 16)

            for L in range(2):
                if L == 1:
                    for qb in range(1, NT):
                        pool.wait_ge(dots_used, qb * IH)
                        d = score[qb][:, qb * P:(qb + 1) * P]
                        pool.affine_select(out=d, in_=d, compare_op=ALU.is_ge, fill=BIG, base=0,
                                           pattern=[[-1, P]], channel_multiplier=1).then_inc(causal, 1)
                        if qb == 1:
                            line.link(pool.memset(masks[0], 0.0))
                            pool.affine_select(out=masks[0][:, 0:P], in_=masks[0][:, 0:P], compare_op=ALU.is_ge, fill=BIG,
                                               base=0, pattern=[[-1, P]], channel_multiplier=1).then_inc(causal, 1)
                for t in range(NT):
                    pool.wait_ge(x_inv, L * NT + t + 1)
                    scale_rows(P_sb[L][:, t % 2], small[:, 32 + 4 * (t % 2):36 + 4 * (t % 2)], XH, M).then_inc(x_prob, 1)
                if L == 1:
                    for n, (qb, g) in enumerate(attention_groups()):
                        pool.wait_ge(l_inv, n + 1)
                        pool.wait_ge(l_exp, 4 * (n + 1))
                        scale_rows(P_sb[1][:, n % 2], small[:, 64 + 4 * (n % 2):68 + 4 * (n % 2)], 4, (qb + 1) * P).then_inc(l_prob, 1)
                pool.wait_ge(tab_zero, 32)
                pool.wait_ge(routed, L + 1)
                for k in range(2):
                    for t in range(NT):
                        pool.indirect_dma_start(out=scratch_tab[L], out_offset=bass.IndirectOffsetOnAxis(ap=dest[:, k, t:t + 1], axis=0),
                                                in_=pay[:, k, t, :], in_offset=None).then_inc(scattered, 16)
                pool.wait_ge(tab_loaded, 32 * (L + 1))
                pool.wait_ge(xn_stored, 16 * NT * (L + 1))
                N = (NE + 1) * L
                for e in range(3):
                    if L and e == 0:
                        pool.wait_ge(moe_done, L)
                    gather(L, e, e, N + e, True)
                with pool.Fori(0, (NE + 1) // 3 - 1) as i:
                    for j in range(3):
                        gather(L, i * 3 + (3 + j), j, i * 3 + (N + 3 + j), False)
                o = ov[L]
                pool.wait_ge(ld["ovl"], 16 * (L + 1))
                n_ov = pool.value_load(ov_n[0:1, 0:1], min_val=0, max_val=OVMAX)
                with pool.If(n_ov > 0):
                    pool.wait_ge(m["xt_psum"], (NE + 1) * (L + 1))
                    with pool.Fori(0, n_ov) as i:
                        wait_alone(pool, o["cur"], i * 32 + 32)
                        pool.tensor_copy(ov_idx[:], ov_cur[0:CAP, 0:1]).then_inc(o["idx"], 1)
                        wait_alone(pool, o["idx"], i + 1)
                        pool.indirect_dma_start(out=xg[0], out_offset=None, in_=scratch_xn[L],
                                                in_offset=bass.IndirectOffsetOnAxis(ap=ov_idx[:], axis=0),
                                                bounds_check=S - 1, oob_is_err=False).then_inc(o["gathered"], 16)
                        wait_alone(pool, o["xt_psum"], i + 1)

        @block.scalar
        def _(act):
            line = Line(act, act_line)
            for n, name in enumerate(("mem_norm", "norm_mix", "norm_ffn")):
                act.dma_start(gains[:, n:6:3, :], a[name].rearrange("l (p k) -> p l k", k=KD)).then_inc(ld["gains"], 16)
            prm_src = ([(R_CW, CONV * NC, a["lru_conv_w"][0].rearrange("k (c p) -> (k c) p", p=P)),
                        (R_CB, NC, a["lru_conv_b"].rearrange("a (c p) -> (a c) p", p=P)),
                        (R_BA, NC, a["lru_b_a"].rearrange("a (c p) -> (a c) p", p=P)),
                        (R_BX, NC, a["lru_b_x"].rearrange("a (c p) -> (a c) p", p=P)),
                        (R_LAM, NC, a["lru_lambda"].rearrange("a (c p) -> (a c) p", p=P))])
            for r, n, src in prm_src:
                act.dma_start(prm_rows[r:r + n, :], src).then_inc(ld["prm"], 16)
            for n, src in enumerate((a["xq_norm"], a["xk_norm"])):
                for h in range(2):
                    act.dma_start(prm_rows[R_XQ + 2 * n:R_XQ + 2 * n + 2, h * HD:(h + 1) * HD], src).then_inc(ld["prm"], 16)
            for n, src in enumerate((a["dsa_q_norm"], a["dsa_k_norm"])):
                for h in range(2):
                    act.dma_start(prm_rows[R_XQ + 4 + n:R_XQ + 5 + n, h * HD:(h + 1) * HD], src).then_inc(ld["prm"], 16)
            act.dma_start(bucket_oh, onehot_dram.ap()).then_inc(ld["onehot"], 16)
            act.dma_start(bucket_bias, a["rel_bias"]).then_inc(ld["onehot"], 16)
            for n, name in enumerate(("moe_b_group", "moe_b_router")):
                c0, c1 = ((0, NG), (NG, R))[n]
                act.dma_start(b_route[:, :, c0:c1], a[name].unsqueeze(0).to_broadcast([P, 2, c1 - c0])).then_inc(ld["broute"], 16)
            act.wait_ge(consts, 1)

            def row_norm(L, kind, n, src, junk, ready):
                for t in range(n):
                    ready(t)
                    k = rows[L, kind, t]
                    c = small[:, k % 8:k % 8 + 1]
                    if k > 8:
                        act.wait_ge(rows_normed, k - 8)
                    line.link(act.activation(junk(t), src(t), ACT.Square, accum_out=c))
                    act.activation(c, c, ACT.Sqrt, bias=eps[:, 0:1], scale=1.0 / D).then_inc(row_sums, 1)

            def raw(L, name, dst, width=512, square=True):
                wait_filled(act, f"{L}.{name}")
                act.activation(dst, bank(f"{L}.{name}")[:, 0:width], ACT.Copy).then_inc(emptied["act"], 1)

            def squares(key, dst, jobs_read):
                n = feats[key]
                if n > 2:
                    k2 = [f for f, v in feats.items() if v == n - 2][0]
                    wait_filled(act, k2[0] + ".sq" + k2[1:])
                for jn in jobs_read:
                    wait_emptied(act, jn)
                act.activation(sqb[int(key[0])][:, n % 2, :], dst, ACT.Square).then_inc(sq_ready, 1)

            def roots(key):
                n = feats[key]
                jn = key[0] + ".sq" + key[1:]
                wait_filled(act, jn)
                if n > 2:
                    act.wait_ge(feat_normed, n - 2)
                act.activation(rs_view(key), bank(jn), ACT.Sqrt, bias=eps[:, 0:1], scale=1.0 / HD).then_inc(emptied["act"], 1)

            for L in range(2):
                def mem_ready(t):
                    if t == 0:
                        act.wait_ge(ld["mem"], 16 * (L + 1))

                def x_ready(t):
                    if t == 0:
                        act.wait_ge(ld["x"], 16)

                if L:
                    act.wait_ge(moe_done, L)
                row_norm(L, "mem", 2, lambda t: mem[:, t, :], lambda t: xn[:, t, :], mem_ready)
                row_norm(L, "mix", NT, lambda t: x[:, t, :], lambda t: xn[:, t, :], x_ready)
                kraw = memKT[:, :, :].rearrange("p a b -> p (a b)")
                for c in range(2):
                    raw(L, f"memK.{c}", memKT[:, c, :], M)
                for mt in range(2):
                    raw(L, f"memV.{mt}", memV[:, mt, :], XW)
                squares(f"{L}.memK", kraw, [f"{L}.memK.1"])
                if L == 0:
                    wait_filled(act, "params")
                    act.activation(prm[:], bank("params")[:, 0:NPRM], ACT.Copy).then_inc(emptied["act"], 1)
                    for h in range(2):
                        wait_filled(act, f"bias{h}")
                        act.activation(bias_rows[:, h * 320:(h + 1) * 320], bank(f"bias{h}")[0:HEADS, 0:320], ACT.Copy).then_inc(emptied["act"], 1)
                    wait_emptied(act, "bias1")
                    act.dma_start(scratch_bias, bias_rows).then_inc(bias_stored, 16)
                    act.wait_ge(lru_par_d, 1)
                    act.activation(small[:, 112:112 + NC], small[:, 104:104 + NC], ACT.Exp).then_inc(lru_par_a, 1)
                    act.wait_ge(lru_par_d, 2)
                    act.activation(small[:, 128:128 + NC], small[:, 120:120 + NC], ACT.Ln).then_inc(lru_par_a, 1)
                roots(f"{L}.memK")
                if L == 0:
                    def conv_input(c):
                        wait_filled(act, f"0.xs.{c}")
                        act.activation(xs[:, c, CONV - 1:], bank(f"0.xs.{c}"), ACT.Copy).then_inc(emptied["act"], 1)

                    def recurrence(c):
                        b = lru[:, c % 2]
                        wait_filled(act, f"0.ra.{c}")
                        if c >= 2:
                            act.wait_ge(lru_h, c - 1)
                        if c == 0:
                            act.wait_ge(gain_ready, 1)
                            act.wait_ge(feat_normed, feats["0.xq.1"])
                        act.activation(b[:, 0, :], bank(f"0.ra.{c}"), ACT.Tanh, bias=small[:, 80 + c:81 + c], scale=0.5).then_inc(emptied["act"], 1)
                        wait_filled(act, f"0.rx.{c}")
                        act.activation(b[:, 2, :], bank(f"0.rx.{c}"), ACT.Tanh, bias=small[:, 86 + c:87 + c], scale=0.5).then_inc(emptied["act"], 1)
                        act.wait_ge(lru_log, c + 1)
                        act.activation(b[:, 1, :], b[:, 0, :], ACT.Tanh).then_inc(lru_tanh, 1)
                        act.wait_ge(lru_tanh, c + 1)
                        act.activation(b[:, 0, :], b[:, 0, :], ACT.Exp).then_inc(lru_exp, 1)
                        act.wait_ge(lru_exp, c + 1)
                        act.activation(xs[:, c, 0:S], b[:, 0, :], ACT.Square).then_inc(lru_sq, 1)
                        act.wait_ge(lru_var, c + 1)
                        act.activation(b[:, 1, :], b[:, 1, :], ACT.Sqrt, scale=-1.0).then_inc(lru_root, 1)

                    for what, c in lru_order():
                        if what == "rec":
                            recurrence(c)
                        elif what == "gate":
                            wait_filled(act, f"0.gate.{c}")
                            act.activation(mix[:, c, :], bank(f"0.gate.{c}"), ACT.Gelu_apprx_tanh).then_inc(emptied["act"], 1)
                        else:
                            conv_input(c)
                            if c == 2:
                                for q in range(2):
                                    raw(0, f"xq.{q}", xqT[0][:, q, :])
                                    squares(f"0.xq.{q}", xqT[0][:, q, :], [f"0.xq.{q}"])
                                for q in range(2):
                                    roots(f"0.xq.{q}")
                else:
                    raw(1, "ki", kiT)
                    squares("1.ki", kiT, ["1.ki"])
                    raw(1, "qi.0", qiT[:, 0, :])
                    roots("1.ki")
                    raw(1, "qi.1", qiT[:, 1, :])
                    wait_filled(act, "1.v")
                    act.activation(v_sb[:, :, :], bank("1.v").rearrange("p (t n) -> p t n", t=NT), ACT.Copy).then_inc(emptied["act"], 1)
                    wait_filled(act, "1.wi")
                    act.activation(wi_sb[:, :, :], bank("1.wi")[:, 0:NT * IH].rearrange("p (t n) -> p t n", t=NT), ACT.Copy,
                                   scale=HD ** -0.5 * IH ** -0.5).then_inc(emptied["act"], 1)
                    for qb in range(1, NT):
                        n = (qb + 1) * P
                        for h in range(IH):
                            jn = f"1.dot.{qb}.{h}"
                            k = (qb - 1) * IH + h
                            wait_filled(act, jn)
                            if k >= 3:
                                act.wait_ge(dots_used, k - 2)
                            act.activation(relu[:, k % 3, 0:n], bank(jn)[:, 0:n], ACT.Relu).then_inc(emptied["act"], 1)
                    last = None
                    for name in ["k"] + [f"q.{c}" for c in range(NC)] + ["xq.0", "xq.1"]:
                        dst = kT if name == "k" else qT[:, int(name[2:]), :] if name[0] == "q" else xqT[1][:, int(name[3:]), :]
                        raw(1, name, dst)
                        squares(f"1.{name}", dst, [f"1.{name}"])
                        if last:
                            roots(f"1.{last}")
                        last = name
                    roots(f"1.{last}")
                for t in range(NT + 1):
                    if t < NT:
                        b = P_sb[L][:, t % 2]
                        if t >= 2:
                            act.wait_ge(filled, jobs.number[f"{L}.xp.{t - 2}.1"] + 1)
                        act.wait_ge(x_max, L * NT + t + 1)
                        for h in range(XH):
                            jn = f"{L}.xl.{t}.{h % 2}"
                            ins = act.activation(b[:, h, 0:M], bank(jn)[:, (h // 2) * M:(h // 2 + 1) * M], ACT.Exp,
                                                 bias=small[:, 16 + 4 * (t % 2) + h:17 + 4 * (t % 2) + h],
                                                 accum_out=small[:, 24 + 4 * (t % 2) + h:25 + 4 * (t % 2) + h])
                            if h >= 2:
                                ins.then_inc(emptied["act"], 1)
                    if t:
                        jn = f"{L}.xp.{t - 1}.0"
                        wait_filled(act, jn)
                        if t >= 3:
                            wait_filled(act, f"{L}.xo.{t - 3}")
                        act.activation(PT_sb[L][:, (t - 1) % 2, 0, :], bank(jn), ACT.Copy).then_inc(emptied["act"], 1)
                if L == 1:
                    gs = attention_groups()
                    for n in range(len(gs) + 1):
                        if n < len(gs):
                            qb, g = gs[n]
                            w = (qb + 1) * P
                            act.wait_ge(l_max, n + 1)
                            for h in range(4):
                                b = P_sb[1][:, n % 2, h, 0:w]
                                act.activation(b, b, ACT.Exp, bias=small[:, 48 + 4 * (n % 2) + h:49 + 4 * (n % 2) + h],
                                               accum_out=small[:, 56 + 4 * (n % 2) + h:57 + 4 * (n % 2) + h]).then_inc(l_exp, 1)
                        if n:
                            qb, g = gs[n - 1]
                            for s in range(qb + 1):
                                if pt_reader(qb, g, s) == "act":
                                    jn = f"1.pt.{qb}.{g}.{s}"
                                    wait_filled(act, jn)
                                    act.activation(PT_sb[1][:, (n - 1) % 2, s, :], bank(jn), ACT.Copy).then_inc(emptied["act"], 1)
                            jn = f"1.pv.{qb}.{g}"
                            wait_filled(act, jn)
                            act.activation(oT[:, (n - 1) % 2, :], bank(jn), ACT.Copy).then_inc(emptied["act"], 1)
                row_norm(L, "ffn", NT, lambda t: x[:, t, :], lambda t: xn_ffn[:, t, :],
                         lambda t: wait_emptied(act, f"{L}.out.{t}.1"))
                act.wait_ge(r_diff, 2 * L + 1)
                act.activation(small[:, 160:160 + NT * NG], small[:, 160:160 + NT * NG], ACT.Exp).then_inc(r_exp, 1)
                act.wait_ge(r_diff, 2 * L + 2)
                act.activation(small[:, 184:184 + NT], small[:, 184:184 + NT], ACT.Exp).then_inc(r_exp, 1)

                def split(q, n):
                    for h in range(2):
                        ins = act.activation(y_hm[h][HALF[h], :], ps[HALF[h], 3, :], ACT.Copy)
                        ins.then_inc(q["y_high"], 1)
                    for h in range(2):
                        act.wait_ge(q["y_rest"], n * 2 + (1 + h))
                        act.activation(y_hm[h][HALF[1 - h], :], y_rest[HALF[1 - h], :], ACT.Copy).then_inc(q["y_mid"], 1)

                def expert(n, first=False):
                    act.wait_ge(m["gu_psum"], n + 1)
                    act.activation(silu[CAP:2 * CAP, :], ps[0:CAP, 1, :], ACT.Silu).then_inc(m["silu_done"], 1)
                    act.wait_ge(m["ht_psum"], n + 1)
                    act.activation(hT, ps[:, 2, 0:KF * CAP].rearrange("p (j n) -> p j n", j=KF), ACT.Copy).then_inc(m["ht_sbuf"], 1)
                    act.wait_ge(m["y_psum"], n + 1)
                    if not first:
                        act.wait_ge(m["c_psum"], n * NT)
                    split(m, n)

                expert(NE * L, first=L == 0)
                with act.Fori(1, NE) as i:
                    expert(i + NE * L)
                o = ov[L]
                act.wait_ge(ld["ovl"], 16 * (L + 1))
                n_ov = act.value_load(ov_n[0:1, 0:1], min_val=0, max_val=OVMAX)
                with act.If(n_ov > 0):
                    act.wait_ge(m["c_psum"], NT * NE * (L + 1))
                    with act.Fori(0, n_ov) as i:
                        act.wait_ge(o["gu_psum"], i + 1)
                        act.activation(silu[CAP:2 * CAP, :], ps[0:CAP, 1, :], ACT.Silu).then_inc(o["silu_done"], 1)
                        act.wait_ge(o["ht_psum"], i + 1)
                        act.activation(hT, ps[:, 2, 0:KF * CAP].rearrange("p (j n) -> p j n", j=KF), ACT.Copy).then_inc(o["ht_sbuf"], 1)
                        act.wait_ge(o["y_psum"], i + 1)
                        split(o, i)

        @block.tensor
        def _(pe):
            state = {"n": 0}

            def open_bank(name):
                n = jobs.number[name]
                assert n == state["n"], (name, n, state)
                state["n"] += 1
                if n >= 8:
                    who = jobs.reader[n - 8]
                    pe.wait_ge(emptied[who], jobs.before[n - 8][who])
                return ps[:, n % 8, :]

            def product(name, pairs, cols=slice(0, 512), part=slice(0, P), close=True, b=None):
                b = open_bank(name) if b is None else b
                for i, (l, r) in enumerate(pairs):
                    ins = pe.matmul(b[part, cols], l, r, start=i == 0, stop=i == len(pairs) - 1)
                if close:
                    ins.then_inc(filled, 1)
                return b

            def transposes(name, src, parts=P, n=4, first=0, step=KD):
                b = open_bank(name)
                for k in range(n):
                    ins = pe.transpose(b[:, k * P:(k + 1) * P], src[:, first + k::step][:, 0:P], ident[:])
                ins.then_inc(filled, 1)

            def norm_sum(key):
                n = feats[key]
                pe.wait_ge(sq_ready, n)
                product(key[0] + ".sq" + key[1:], [(ones_head[:], sqb[int(key[0])][:, n % 2, :])])

            pe.wait_ge(consts, 1)
            for L in range(2):
                for mt in range(2):
                    pe.wait_ge(rows_normed, rows[L, "mem", mt])
                    for h in range(2):
                        transposes(f"{L}.memT.{mt}.{h}", mem[:, mt, :], first=4 * h)
                pe.wait_ge(ld["wkv"], 16 * (L + 1))
                wait_emptied(pe, f"{L}.memT.1.1")
                for c in range(2):
                    product(f"{L}.memK.{c}", [(w_kv[:, k, c * P:(c + 1) * P], memT[:, k, :]) for k in range(KD)], cols=slice(0, M))
                for mt in range(2):
                    product(f"{L}.memV.{mt}", [(memT[:, k, mt * P:(mt + 1) * P], w_kv[:, k, XW:2 * XW]) for k in range(KD)],
                            cols=slice(0, XW))
                if L == 0:
                    pe.wait_ge(ld["prm"], 16 * 13)
                    b = open_bank("params")
                    pe.transpose(b[:, 0:NPRM], prm_rows[:, :], ident[0:NPRM, 0:NPRM]).then_inc(filled, 1)
                    pe.wait_ge(ld["onehot"], 32)
                    for h in range(2):
                        product(f"bias{h}", [(bucket_bias, bucket_oh[:, h * 320:(h + 1) * 320])],
                                cols=slice(0, 320), part=slice(0, HEADS))
                for t in range(NT):
                    pe.wait_ge(rows_normed, rows[L, "mix", t])
                    for h in range(2):
                        transposes(f"{L}.xT.{t}.{h}", xn[:, t, :], first=4 * h)
                norm_sum(f"{L}.memK")
                pe.wait_ge(ld["win"], 16 * (L + 1))
                wait_emptied(pe, f"{L}.xT.{NT - 1}.1")

                def project(name, c0, width=P):
                    product(f"{L}.{name}", [(w_in[L][:, k, c0:c0 + width], xT[:, k, :]) for k in range(KD)])

                def project_twice(name, c0):
                    b = open_bank(f"{L}.{name}")
                    for k in range(KD):
                        for h in range(2):
                            ins = pe.matmul(b[h * HD:(h + 1) * HD, :], w_in[L][:, k, c0:c0 + HD], xT[:, k, :],
                                            start=k == 0, stop=k == KD - 1)
                    ins.then_inc(filled, 1)

                if L == 0:
                    def block_gates(c):
                        if c == 0:
                            pe.wait_ge(ld["wg"], 16 * 16)
                        pair, r = c // 3, c % 3
                        for g, nm in ((0, "ra"), (1, "rx")):
                            w = gate_w[:, g, pair]
                            x0, x1, x2 = (xc[:, 3 * pair + q, :] for q in range(3))
                            pe.wait_ge(xc_ready, 3 * pair + (2 if r == 0 else 3))
                            b = open_bank(f"0.{nm}.{c}")
                            if r == 0:
                                todo = [(slice(0, P), 0, slice(0, P))]
                            elif r == 1:
                                todo = [(slice(0, 64), 0, slice(P, LB)), (slice(64, P), 1, slice(0, 64))]
                            else:
                                todo = [(slice(0, P), 1, slice(64, LB))]
                            for part, odd, cols in todo:
                                if odd == 0:
                                    terms = [(w[:, 0, cols], x0), (w[0:64, 1, cols], x1[0:64])]
                                else:
                                    terms = [(w[64:P, 1, cols], x1[64:P]), (w[:, 2, cols], x2)]
                                for i, (l, rr) in enumerate(terms):
                                    ins = pe.matmul(b[part, :], l, rr, start=i == 0, stop=i == 1)
                            ins.then_inc(filled, 1)

                    for what, c in lru_order():
                        if what == "rec":
                            block_gates(c)
                        elif what == "gate":
                            if c == 0:
                                pe.wait_ge(ld["wing"], 16)
                            project(f"gate.{c}", LRU + c * P)
                        else:
                            project(f"xs.{c}", c * P)
                            if c == 2:
                                pe.wait_ge(ld["winq"], 16)
                                project("xq.0", 2 * LRU)
                                project("xq.1", 2 * LRU + P)
                                norm_sum("0.xq.0")
                                norm_sum("0.xq.1")
                else:
                    project_twice("ki", C_KI)
                    project("qi.0", C_QI)
                    norm_sum("1.ki")
                    project("qi.1", C_QI + P)
                    for nm, c0, w in (("v", C_V, VD), ("wi", C_WI, IH)):
                        b = open_bank(f"1.{nm}")
                        for t in range(NT):
                            for k in range(KD):
                                ins = pe.matmul(b[:, t * w:(t + 1) * w], xT[:, k, t * P:(t + 1) * P], w_in[1][:, k, c0:c0 + w],
                                                start=k == 0, stop=k == KD - 1)
                        ins.then_inc(filled, 1)
                    wait_emptied(pe, "1.qi.1")
                    pe.wait_ge(feat_normed, feats["1.ki"])
                    for qb in range(1, NT):
                        for h in range(IH):
                            r0 = slice((h % 2) * HD, (h % 2) * HD + HD)
                            product(f"1.dot.{qb}.{h}", [(qiT[r0, h // 2, qb * P:(qb + 1) * P], kiT[r0, 0:(qb + 1) * P])],
                                    cols=slice(0, (qb + 1) * P))
                    last = None
                    for name, c0 in [("k", C_K)] + [(f"q.{c}", C_Q + c * P) for c in range(NC)] + [("xq.0", C_XQ), ("xq.1", C_XQ + P)]:
                        if name == "k":
                            project_twice("k", C_K)
                        else:
                            project(name, c0)
                        if last:
                            norm_sum(f"1.{last}")
                        last = name
                    norm_sum(f"1.{last}")

                for t in range(NT + 1):
                    if t < NT:
                        if t == 0:
                            pe.wait_ge(feat_normed, feats[f"{L}.xq.1"])
                        bs = [open_bank(f"{L}.xl.{t}.{par}") for par in range(2)]
                        for h in range(XH):
                            r0 = slice((h % 2) * HD, (h % 2) * HD + HD)
                            ins = pe.matmul(bs[h % 2][:, (h // 2) * M:(h // 2 + 1) * M], xqT[L][r0, h // 2, t * P:(t + 1) * P],
                                            memKT[r0, h // 2, :], start=True, stop=True)
                            if h >= 2:
                                ins.then_inc(filled, 1)
                    if t:
                        tt = t - 1
                        pe.wait_ge(x_prob, L * NT + tt + 1)
                        for mt in range(2):
                            b = open_bank(f"{L}.xp.{tt}.{mt}")
                            for h in range(XH):
                                ins = pe.transpose(b[:, h * P:(h + 1) * P], P_sb[L][:, tt % 2, h, mt * P:(mt + 1) * P], ident[:])
                            ins.then_inc(filled, 1)
                        b = open_bank(f"{L}.xo.{tt}")
                        wait_emptied(pe, f"{L}.xp.{tt}.0")
                        wait_emptied(pe, f"{L}.xp.{tt}.1")
                        for h in range(XH):
                            for mt in range(2):
                                ins = pe.matmul(b[(h % 2) * HD:(h % 2) * HD + HD, (h // 2) * P:(h // 2 + 1) * P],
                                                memV[:, mt, h * HD:(h + 1) * HD], PT_sb[L][:, tt % 2, mt, h * P:(h + 1) * P],
                                                start=mt == 0, stop=mt == 1)
                        ins.then_inc(filled, 1)
                if L == 1:
                    gs = attention_groups()
                    for n in range(len(gs) + 1):
                        if n < len(gs):
                            qb, g = gs[n]
                            w = (qb + 1) * P
                            if g == 0:
                                if qb == 0:
                                    pe.wait_ge(causal, 2)
                                else:
                                    pe.wait_ge(masked, qb)
                            bs = [open_bank(f"1.l.{qb}.{g}.{h}") for h in range(4)]
                            for h in range(4):
                                pe.matmul(bs[h][:, 0:w], identb[:], masks[qb][:, 0:w], start=True, stop=False)
                            for h in range(4):
                                hh = 4 * g + h
                                r0 = slice((hh % 2) * HD, (hh % 2) * HD + HD)
                                pe.matmul(bs[h][:, 0:w], qT[r0, hh // 2, qb * P:(qb + 1) * P], kT[r0, 0:w],
                                          start=False, stop=True).then_inc(filled, 1)
                        if n:
                            qb, g = gs[n - 1]
                            b_ = (n - 1) % 2
                            pe.wait_ge(l_prob, n)
                            for s in range(qb + 1):
                                b = open_bank(f"1.pt.{qb}.{g}.{s}")
                                for h in range(4):
                                    ins = pe.transpose(b[:, h * P:(h + 1) * P], P_sb[1][:, b_, h, s * P:(s + 1) * P], ident[:])
                                ins.then_inc(filled, 1)
                            b = open_bank(f"1.pv.{qb}.{g}")
                            for s in range(qb + 1):
                                wait_emptied(pe, f"1.pt.{qb}.{g}.{s}")
                                ins = pe.matmul(b, v_sb[:, s, :], PT_sb[1][:, b_, s, :], start=s == 0, stop=s == qb)
                            ins.then_inc(filled, 1)
                            b = open_bank(f"1.uv.{qb}.{g}")
                            wait_emptied(pe, f"1.pv.{qb}.{g}")
                            if n == 1:
                                pe.wait_ge(ld["wuv"], 16)
                            for h in range(4):
                                hh = 4 * g + h
                                ins = pe.matmul(b[(hh % 2) * HD:(hh % 2) * HD + HD, (h // 2) * P:(h // 2 + 1) * P],
                                                w_uv[:, hh, :], oT[:, b_, h * P:(h + 1) * P], start=True, stop=True)
                            ins.then_inc(filled, 1)
                pe.wait_ge(ld["wout"], 16 * (L + 1))
                wait_emptied(pe, f"{L}.xo.{NT - 1}")
                if L == 0:
                    pe.wait_ge(lru_y, NC)
                else:
                    wait_emptied(pe, f"1.uv.{NT - 1}.{HEADS // 4 - 1}")
                for t in range(NT):
                    for h in range(2):
                        product(f"{L}.out.{t}.{h}", [(mix[:, c, t * P:(t + 1) * P], w_out[:, c, h * 512:(h + 1) * 512]) for c in range(8)])
                for t in range(NT):
                    pe.wait_ge(rows_normed, rows[L, "ffn", t])
                    for h in range(2):
                        transposes(f"{L}.fT.{t}.{h}", xn_ffn[:, t, :], first=4 * h)
                pe.wait_ge(ld["wr"], 32 * (L + 1))
                b = open_bank(f"{L}.route")
                for t in range(NT):
                    wait_emptied(pe, f"{L}.fT.{t}.1")
                    for k in range(KD):
                        ins = pe.matmul(b[:, t * R:(t + 1) * R], xT[:, k, t * P:(t + 1) * P], w_route[:, k, :],
                                        start=k == 0, stop=k == KD - 1)
                ins.then_inc(filled, 1)
                b = open_bank(f"{L}.rank")
                pe.wait_ge(chosen, 2 * L + 1)
                for t in range(NT):
                    for u in range(t + 1):
                        pe.matmul(b[:, t * NE:(t + 1) * NE], before[:] if u == t else ones_b[:], choice[:, u, :],
                                  start=u == 0, stop=u == t)
                for u in range(NT):
                    ins = pe.matmul(b[:, NT * NE:(NT + 1) * NE], ones_b[:], choice[:, u, :], start=u == 0, stop=u == NT - 1)
                ins.then_inc(filled, 1)
                for n in range(state["n"] - 8, state["n"]):
                    who = jobs.reader[n]
                    pe.wait_ge(emptied[who], jobs.before[n][who])

                def tokens_T(src, s_):
                    for k in range(KD):
                        ins = pe.transpose(ps[:, 0, k * CAP:(k + 1) * CAP], src[:, k::KD][:, 0:P], ident[0:CAP, 0:CAP])
                    ins.then_inc(s_, 1)

                def gate_up(slot, s_):
                    wg, wu, _ = slots[slot]
                    for k in range(KD):
                        pe.matmul(ps[0:CAP, 1, :], tokT[:, k, :], wg[:, k, :], start=k == 0, stop=k == KD - 1)
                        ins = pe.matmul(ps[CAP:P, 1, :], tokT[:, k, :], wu[:, k, :], start=k == 0, stop=k == KD - 1)
                    ins.then_inc(s_, 1)

                def hidden_T(s_):
                    for j in range(KF):
                        ins = pe.transpose(ps[:, 2, j * CAP:(j + 1) * CAP], h_sb[0:CAP, j::KF][:, 0:P], ident[0:CAP, 0:CAP])
                    ins.then_inc(s_, 1)

                def down(slot, s_):
                    wd = slots[slot][2]
                    for j in range(KF):
                        pe.matmul(ps[0:CAP, 3, :], hT[:, j, :], wd[:, j, 0:512], start=j == 0, stop=j == KF - 1)
                        ins = pe.matmul(ps[CAP:P, 3, :], hT[:, j, :], wd[:, j, 512:D], start=j == 0, stop=j == KF - 1)
                    ins.then_inc(s_, 1)

                def combine(t, s_):
                    for h in range(2):
                        b = ps[:, 4 + 2 * (t % 2) + h, :]
                        lo = HALF[1 - h]
                        pe.matmul(b, onehot[:, t * P:(t + 1) * P], y_hm[h], start=True, stop=False)
                        ins = pe.matmul(b, onehot[lo, t * P:(t + 1) * P], y_lo[lo, :], start=False, stop=True)
                    ins.then_inc(s_, 1)

                def combine_of(n, ts, started=True):
                    for t in ts:
                        if t == 0:
                            pe.wait_ge(m["y_mid"], n * 2 + 2)
                            pe.wait_ge(m["y_low"], n * 2 + 2)
                            pe.wait_ge(m["g_done"], n + 1)
                        if started or t >= 2:
                            pe.wait_ge(m["c_added"], n * NT + (t - 1))
                        combine(t, m["c_psum"])

                def expert(n, slot, landed, gath, first=False, second=False):
                    pe.wait_ge(gu_landed[slot], landed * 32)
                    pe.wait_ge(m["xt_sbuf"], n + (L + 1))
                    gate_up(slot, m["gu_psum"])
                    if not first:
                        combine_of(n + (-1), (0, 1), not second)
                    wait_alone(pe, m["h_done"], n + 1)
                    hidden_T(m["ht_psum"])
                    wait_alone(pe, gathered[(slot + 1) % NS], gath * 16)
                    tokens_T(xg[(slot + 1) % NS], m["xt_psum"])
                    pe.wait_ge(m["ht_sbuf"], n + 1)
                    pe.wait_ge(d_landed[slot], landed * 16)
                    down(slot, m["y_psum"])
                    if not first:
                        combine_of(n + (-1), (2, 3))

                base = slot_base[L]
                gb = 11 * L
                n0 = NE * L
                pe.wait_ge(gathered[0], 16 * (gb + 1))
                tokens_T(xg[0], m["xt_psum"])
                expert(n0, 0, base[0] + 1, gb + 1, first=True)
                expert(n0 + 1, 1, base[1] + 1, gb + 1, second=L == 0)
                with pe.Fori(0, (NE - 2) // 3) as i:
                    expert(i * 3 + (n0 + 2), 2, i + (base[2] + 1), i + (gb + 2))
                    expert(i * 3 + (n0 + 3), 0, i + (base[0] + 2), i + (gb + 2))
                    expert(i * 3 + (n0 + 4), 1, i + (base[1] + 2), i + (gb + 2))
                combine_of(n0 + NE - 1, (0, 1, 2, 3))
                o = ov[L]
                pe.wait_ge(ld["ovl"], 16 * (L + 1))
                n_ov = pe.value_load(ov_n[0:1, 0:1], min_val=0, max_val=OVMAX)
                with pe.If(n_ov > 0):
                    pe.wait_ge(m["c_added"], NT * (n0 + NE))
                    pe.wait_ge(m["xt_sbuf"], (NE + 1) * (L + 1))
                    with pe.Fori(0, n_ov) as i:
                        wait_alone(pe, o["gathered"], i * 16 + 16)
                        tokens_T(xg[0], o["xt_psum"])
                        pe.wait_ge(o["xt_sbuf"], i + 1)
                        pe.wait_ge(o["landed"], i * 48 + 48)
                        gate_up(0, o["gu_psum"])
                        wait_alone(pe, o["h_done"], i + 1)
                        hidden_T(o["ht_psum"])
                        pe.wait_ge(o["ht_sbuf"], i + 1)
                        down(0, o["y_psum"])
                        pe.wait_ge(o["y_mid"], i * 2 + 2)
                        pe.wait_ge(o["y_low"], i * 2 + 2)
                        pe.wait_ge(o["g_done"], i + 1)
                        for t in range(NT):
                            if t >= 2:
                                pe.wait_ge(o["c_added"], i * NT + (t - 1))
                            combine(t, o["c_psum"])
                        wait_alone(pe, o["c_added"], i * NT + NT)
                pe.wait_ge(moe_done, L + 1)

        @block.vector
        def _(dve):
            line = Line(dve, dve_line)

            def rows_normalise(L, kind, n, src, dst, ready=lambda t: None):
                for t in range(n):
                    k = rows[L, kind, t]
                    c = small[:, k % 8:k % 8 + 1]
                    r = small[:, 8 + k % 8:9 + k % 8]
                    dve.wait_ge(row_sums, k)
                    ready(t)
                    line.link(dve.reciprocal(r, c))
                    dve.tensor_scalar(dst(t), src(t), r, None, ALU.mult).then_inc(rows_normed, 1)
                    dve.wait_ge(rows_normed, k)

            def features_normalise(key, dst, gain):
                n = feats[key]
                wait_emptied(dve, key[0] + ".sq" + key[1:])
                r = rs_view(key)
                line.link(dve.reciprocal(r, r))
                dve.scalar_tensor_tensor(out=dst, in0=dst, scalar=gain, in1=r, op0=ALU.mult, op1=ALU.mult).then_inc(feat_normed, 1)

            def spread_gain(name, dst, g, h, width):
                wait_filled(dve, name)
                dve.tensor_tensor(dst, bank(name).rearrange("p (k n) -> p k n", k=4)[:, :, 0:width],
                                  gains[:, g, 4 * h:4 * h + 4].unsqueeze(2).to_broadcast([P, 4, width]), ALU.mult)\
                   .then_inc(emptied["dve"], 1)

            one = small[:, 155:156]
            dve.wait_ge(consts, 1)

            for L in range(2):
                rows_normalise(L, "mem", 2, lambda t: mem[:, t, :], lambda t: mem[:, t, :])
                if L == 0:
                    dve.wait_ge(ld["gains"], 48)
                for mt in range(2):
                    for h in range(2):
                        spread_gain(f"{L}.memT.{mt}.{h}", memT[:, 4 * h:4 * h + 4, mt * P:(mt + 1) * P], 3 * L, h, P)
                rows_normalise(L, "mix", NT, lambda t: x[:, t, :], lambda t: xn[:, t, :])
                for t in range(NT):
                    for h in range(2):
                        spread_gain(f"{L}.xT.{t}.{h}", xT[:, 4 * h:4 * h + 4, t * P:(t + 1) * P], 3 * L + 1, h, P)
                if L == 0:
                    wait_emptied(dve, "params")
                    lam = prm[:, R_LAM:R_LAM + NC]
                    line.link(dve.tensor_scalar(small[:, 104:104 + NC], lam, -1.0, None, ALU.mult))
                    line.link(dve.tensor_tensor(small[:, 96:96 + NC], small[:, 104:104 + NC], lam, ALU.max))
                    dve.tensor_scalar(small[:, 104:104 + NC], small[:, 96:96 + NC], -1.0, None, ALU.mult).then_inc(lru_par_d, 1)
                    dve.wait_ge(lru_par_a, 1)
                    dve.tensor_scalar(small[:, 120:120 + NC], small[:, 112:112 + NC], 1.0, None, ALU.add).then_inc(lru_par_d, 1)
                    dve.wait_ge(lru_par_d, 2)
                    line.link(dve.tensor_scalar(small[:, 96:96 + NC], small[:, 120:120 + NC], -1.0, None, ALU.add))
                    line.link(dve.tensor_scalar(small[:, 136:136 + NC], small[:, 96:96 + NC], 0.0, None, ALU.is_equal))
                    line.link(dve.tensor_tensor(small[:, 96:96 + NC], small[:, 96:96 + NC], small[:, 136:136 + NC], ALU.add))
                    line.link(dve.reciprocal(small[:, 96:96 + NC], small[:, 96:96 + NC]))
                    dve.wait_ge(lru_par_a, 2)
                    line.link(dve.tensor_tensor(small[:, 136:136 + NC], small[:, 136:136 + NC], small[:, 128:128 + NC], ALU.add))
                    line.link(dve.tensor_tensor(small[:, 136:136 + NC], small[:, 136:136 + NC], small[:, 96:96 + NC], ALU.mult))
                    line.link(dve.tensor_tensor(small[:, 136:136 + NC], small[:, 136:136 + NC], small[:, 112:112 + NC], ALU.mult))
                    line.link(dve.tensor_scalar(small[:, 96:96 + NC], lam, -1.0, 0.0, ALU.mult, ALU.max))
                    line.link(dve.tensor_tensor(small[:, 136:136 + NC], small[:, 136:136 + NC], small[:, 96:96 + NC], ALU.add))
                    line.link(dve.tensor_scalar(small[:, 144:144 + NC], small[:, 136:136 + NC], -4.0, None, ALU.mult))
                    line.link(dve.tensor_scalar(prm[:, R_BA:R_BA + 2 * NC], prm[:, R_BA:R_BA + 2 * NC], 0.5, None, ALU.mult))
                    line.link(dve.tensor_copy(small[:, 80:80 + 2 * NC], prm[:, R_BA:R_BA + 2 * NC]))
                    for n, (g0, g1) in enumerate(((R_XQ, R_XQ + 2), (R_XQ + 1, R_XQ + 3), (R_XQ + 4, R_XQ + 5))):
                        line.step(dve.scalar_tensor_tensor(out=small[:, 152 + n:153 + n], in0=prm[:, g0:g0 + 1], scalar=0.125,
                                                           in1=prm[:, g1:g1 + 1], op0=ALU.mult, op1=ALU.mult))
                    line.settle()
                    dve.memset(small[:, 155:156], 1.0).then_inc(gain_ready, 1)
                    dve.wait_ge(gain_ready, 1)
                    dve.wait_ge(ld["broute"], 32)
                features_normalise(f"{L}.memK", memKT[:, :, :].rearrange("p a b -> p (a b)"), small[:, 152 + L:153 + L])
                if L == 0:
                    def convolve(c):
                        wait_emptied(dve, f"0.xs.{c}")
                        line.link(dve.tensor_scalar(xc[:, c, :], xs[:, c, 0:S], prm[:, R_CW + c:R_CW + c + 1],
                                                    prm[:, R_CB + c:R_CB + c + 1], ALU.mult, ALU.add))
                        for k in range(1, CONV):
                            r = R_CW + k * NC + c
                            ins = dve.scalar_tensor_tensor(out=xc[:, c, :], in0=xs[:, c, k:k + S], scalar=prm[:, r:r + 1],
                                                           in1=xc[:, c, :], op0=ALU.mult, op1=ALU.add)
                            if k < CONV - 1:
                                line.link(ins)
                            else:
                                ins.then_inc(xc_ready, 1)
                    def recurrence(c):
                        b = lru[:, c % 2]
                        wait_emptied(dve, f"0.rx.{c}")
                        dve.tensor_scalar(b[:, 0, :], b[:, 0, :], 1.0, small[:, 144 + c:145 + c], ALU.add, ALU.mult).then_inc(lru_log, 1)
                        dve.wait_ge(xc_ready, c + 1)
                        line.step(dve.scalar_tensor_tensor(out=b[:, 2, :], in0=b[:, 2, :], scalar=1.0, in1=xc[:, c, :],
                                                           op0=ALU.add, op1=ALU.mult))
                        dve.wait_ge(lru_sq, c + 1)
                        d = xs[:, c, 0:S]
                        dve.scalar_tensor_tensor(out=b[:, 1, :], in0=d, scalar=1.0, in1=b[:, 1, :], op0=ALU.add, op1=ALU.mult)\
                           .then_inc(lru_var, 1)
                        dve.wait_ge(lru_root, c + 1)
                        line.link(dve.scalar_tensor_tensor(out=b[:, 1, :], in0=b[:, 1, :], scalar=0.5, in1=b[:, 2, :],
                                                           op0=ALU.mult, op1=ALU.mult))
                        dve.tensor_tensor_scan(d, b[:, 0, :], b[:, 1, :], 0.0, ALU.mult, ALU.add).then_inc(lru_h, 1)

                    for what, c in lru_order():
                        if what == "conv":
                            convolve(c)
                            if c == 2:
                                for q in range(2):
                                    features_normalise(f"0.xq.{q}", xqT[0][:, q, :], one)
                        elif what == "rec":
                            recurrence(c)
                    for c in range(NC):
                        dve.wait_ge(lru_h, c + 1)
                        wait_emptied(dve, f"0.gate.{c}")
                        dve.tensor_tensor(mix[:, c, :], mix[:, c, :], xs[:, c, 0:S], ALU.mult).then_inc(lru_y, 1)
                else:
                    features_normalise("1.ki", kiT, one)

                    def scores(qb):
                        n = (qb + 1) * P
                        for h in range(IH):
                            k = (qb - 1) * IH + h
                            wait_emptied(dve, f"1.dot.{qb}.{h}")
                            if h == 0:
                                dve.tensor_scalar(score[qb][:, 0:n], relu[:, k % 3, 0:n], wi_sb[:, qb, 0:1], None, ALU.mult).then_inc(dots_used, 1)
                            else:
                                dve.wait_ge(dots_used, k)
                                dve.scalar_tensor_tensor(out=score[qb][:, 0:n], in0=relu[:, k % 3, 0:n], scalar=wi_sb[:, qb, h:h + 1],
                                                         in1=score[qb][:, 0:n], op0=ALU.mult, op1=ALU.add).then_inc(dots_used, 1)

                    def take_largest(qb):
                        n = (qb + 1) * P
                        dve.wait_ge(causal, qb if qb == 1 else qb + 1)
                        for r in range(TOPK // 8):
                            line.link(dve.max(small[:, 200:208], score[qb][:, 0:n]))
                            line.link(dve.match_replace(score[qb][:, 0:n], small[:, 200:208], score[qb][:, 0:n], TAKEN))
                        dve.tensor_scalar(masks[qb][:, 0:n], score[qb][:, 0:n], TAKEN / 1.5, BIG, ALU.is_gt, ALU.mult).then_inc(masked, 1)

                    for qb in range(1, NT):
                        scores(qb)
                    take_largest(1)
                    features_normalise("1.k", kT, small[:, 154:155])
                    features_normalise("1.q.0", qT[:, 0, :], one)
                    take_largest(2)
                    for c in range(1, 4):
                        features_normalise(f"1.q.{c}", qT[:, c, :], one)
                    take_largest(3)
                    for c in range(4, NC):
                        features_normalise(f"1.q.{c}", qT[:, c, :], one)
                    for c in range(2):
                        features_normalise(f"1.xq.{c}", xqT[1][:, c, :], one)
                for t in range(NT + 1):
                    if t < NT:
                        q4 = 4 * (t % 2)
                        wait_filled(dve, f"{L}.xl.{t}.1")
                        if t >= 2:
                            wait_emptied(dve, f"{L}.xl.{t - 2}.1")
                        for par in range(2):
                            nm = small[:, 16 + q4:20 + q4].rearrange("p (a b) -> p b a", b=2)[:, par, :]
                            ins = dve.tensor_reduce(nm, bank(f"{L}.xl.{t}.{par}").rearrange("p (a n) -> p a n", a=2), AX.X, ALU.max, negate=True)
                            if par:
                                ins.then_inc(x_max, 1)
                        wait_emptied(dve, f"{L}.xl.{t}.1")
                        if t >= 2:
                            dve.wait_ge(x_prob, L * NT + t - 1)
                        dve.reciprocal(small[:, 32 + q4:36 + q4], small[:, 24 + q4:28 + q4]).then_inc(x_inv, 1)
                    if t:
                        tt = t - 1
                        jn = f"{L}.xp.{tt}.1"
                        wait_filled(dve, jn)
                        if tt >= 2:
                            wait_filled(dve, f"{L}.xo.{tt - 2}")
                        dve.tensor_copy(PT_sb[L][:, tt % 2, 1, :], bank(jn)).then_inc(emptied["dve"], 1)
                        jn = f"{L}.xo.{tt}"
                        wait_filled(dve, jn)
                        dve.tensor_copy(mix[:, 6:8, tt * P:(tt + 1) * P], bank(jn)[:, 0:2 * P].rearrange("p (a n) -> p a n", a=2))\
                           .then_inc(emptied["dve"], 1)
                if L == 1:
                    dve.wait_ge(ld["bias"], 16)
                    gs = attention_groups()
                    for n in range(len(gs) + 1):
                        if n < len(gs):
                            qb, g = gs[n]
                            w, q4 = (qb + 1) * P, 4 * (n % 2)
                            if n >= 2:
                                dve.wait_ge(l_exp, 4 * (n - 1))
                                pq, pg = gs[n - 2]
                                wait_filled(dve, f"1.pt.{pq}.{pg}.{pq}")
                            elif n == 0:
                                wait_filled(dve, f"1.xp.{NT - 1}.1")
                            for h in range(4):
                                jn = f"1.l.{qb}.{g}.{h}"
                                wait_filled(dve, jn)
                                dve.tensor_tensor_reduce(out=P_sb[1][:, n % 2, h, 0:w], in0=bank(jn)[:, 0:w],
                                                         in1=T_all[:, 4 * g + h, S - w:S], scale=1.0, scalar=-3.0e38,
                                                         op0=ALU.add, op1=ALU.max, accum_out=small[:, 210 + q4 + h:211 + q4 + h])\
                                   .then_inc(emptied["dve"], 1)
                            wait_emptied(dve, f"1.l.{qb}.{g}.3")
                            dve.tensor_scalar(small[:, 48 + q4:52 + q4], small[:, 210 + q4:214 + q4], -1.0, None, ALU.mult).then_inc(l_max, 1)
                        if n:
                            qb, g = gs[n - 1]
                            for s in range(qb + 1):
                                if pt_reader(qb, g, s) == "dve":
                                    jn = f"1.pt.{qb}.{g}.{s}"
                                    wait_filled(dve, jn)
                                    dve.tensor_copy(PT_sb[1][:, (n - 1) % 2, s, :], bank(jn)).then_inc(emptied["dve"], 1)
                            jn = f"1.uv.{qb}.{g}"
                            wait_filled(dve, jn)
                            dve.tensor_copy(mix[:, 2 * g:2 * g + 2, qb * P:(qb + 1) * P], bank(jn)[:, 0:2 * P].rearrange("p (a n) -> p a n", a=2))\
                               .then_inc(emptied["dve"], 1)
                        if n < len(gs):
                            q4 = 4 * (n % 2)
                            dve.wait_ge(l_exp, 4 * (n + 1))
                            if n >= 2:
                                dve.wait_ge(l_prob, n - 1)
                            dve.reciprocal(small[:, 64 + q4:68 + q4], small[:, 56 + q4:60 + q4]).then_inc(l_inv, 1)
                for t in range(NT):
                    for h in range(2):
                        jn = f"{L}.out.{t}.{h}"
                        wait_filled(dve, jn)
                        xt_ = x[:, t, h * 512:(h + 1) * 512]
                        dve.tensor_tensor(xt_, bank(jn), xt_, ALU.add).then_inc(emptied["dve"], 1)
                rows_normalise(L, "ffn", NT, lambda t: x[:, t, :], lambda t: xn_ffn[:, t, :])
                for t in range(NT):
                    for h in range(2):
                        spread_gain(f"{L}.fT.{t}.{h}", xT[:, 4 * h:4 * h + 4, t * P:(t + 1) * P], 3 * L + 2, h, P)
                rt = route_area
                lg = rt[:, 0:NT * R].rearrange("p (t r) -> p t r", t=NT)
                grp, exl = lg[:, :, 0:NG], lg[:, :, NG:R]
                wait_filled(dve, f"{L}.route")
                dve.tensor_tensor(lg, bank(f"{L}.route")[:, 0:NT * R].rearrange("p (t r) -> p t r", t=NT),
                                  b_route[:, L, :].unsqueeze(1).to_broadcast([P, NT, R]), ALU.add).then_inc(emptied["dve"], 1)
                wait_emptied(dve, f"{L}.route")
                gm = small[:, 218:218 + NT]
                line.link(dve.tensor_reduce(gm, grp, AX.X, ALU.max))
                eg = small[:, 160:160 + NT * NG].rearrange("p (t g) -> p t g", t=NT)
                gmb = gm.unsqueeze(2).to_broadcast([P, NT, NG])
                dve.tensor_tensor(eg, grp, gmb, ALU.subtract).then_inc(r_diff, 1)
                first = rt[:, 160:160 + NT * NG].rearrange("p (t g) -> p t g", t=NT)
                line.link(dve.tensor_tensor(first, grp, gmb, ALU.is_equal))
                line.link(dve.tensor_tensor(first, first, rank_w[:].unsqueeze(1).to_broadcast([P, NT, NG]), ALU.mult))
                fm = small[:, 222:222 + NT]
                line.link(dve.tensor_reduce(fm, first, AX.X, ALU.max))
                line.link(dve.tensor_tensor(first, first, fm.unsqueeze(2).to_broadcast([P, NT, NG]), ALU.is_equal))
                line.link(dve.tensor_scalar(first, first, -BIG, BIG, ALU.mult, ALU.add))
                e4 = exl.rearrange("p t (g e) -> p t g e", g=NG)
                eall = rt[:, 192:192 + NT * NE].rearrange("p (t e) -> p t e", t=NT)
                for t in range(NT):
                    line.step(dve.tensor_tensor(eall[:, t, :].rearrange("p (g e) -> p g e", g=NG), e4[:, t],
                                                first[:, t, :].unsqueeze(2).to_broadcast([P, NG, EG]), ALU.add))
                line.settle()
                for t in range(NT):
                    line.step(dve.max(v8[:, t, :], eall[:, t, :]))
                line.settle()
                for t in range(NT):
                    line.step(dve.max_index(i8[:, t, :], v8[:, t, :], eall[:, t, :]))
                line.settle()
                e2 = small[:, 184:184 + NT]
                dve.tensor_tensor(e2, v8[:, :, 1], v8[:, :, 0], ALU.subtract).then_inc(r_diff, 1)
                idf = small[:, 226:226 + 2 * NT].rearrange("p (t k) -> p t k", k=2)
                line.link(dve.tensor_copy(idf, i8[:, :, 0:2]))
                oh = [rt[:, 320 + 128 * k:448 + 128 * k].rearrange("p (t e) -> p t e", t=NT) for k in range(2)]
                iob = iota_e[:].unsqueeze(1).to_broadcast([P, NT, NE])
                for k in range(2):
                    line.step(dve.tensor_tensor(oh[k], iob, idf[:, :, k:k + 1].to_broadcast([P, NT, NE]), ALU.is_equal))
                line.settle()
                dve.tensor_tensor(choice[:], oh[0], oh[1], ALU.add).then_inc(chosen, 1)
                dve.wait_ge(r_exp, 2 * L + 1)
                sg, g1, g2 = (small[:, 234 + 4 * q:238 + 4 * q] for q in range(3))
                line.link(dve.tensor_reduce(sg, eg, AX.X, ALU.add))
                dve.wait_ge(r_exp, 2 * L + 2)
                line.link(dve.tensor_scalar(g1, e2, 1.0, None, ALU.add))
                line.link(dve.tensor_tensor(g1, g1, sg, ALU.mult))
                line.link(dve.reciprocal(g1, g1))
                if L:
                    dve.wait_ge(scattered, 16 * 2 * NT * L)
                line.link(dve.tensor_copy(pay[:, 0, :, 1], g1))
                line.link(dve.tensor_tensor(pay[:, 1, :, 1], g1, e2, ALU.mult))
                wait_filled(dve, f"{L}.rank")
                row = rt[:, 576:576 + NT * NE].rearrange("p (t e) -> p t e", t=NT)
                line.link(dve.scalar_tensor_tensor(out=row, in0=bank(f"{L}.rank")[:, 0:NT * NE].rearrange("p (t e) -> p t e", t=NT),
                                                   scalar=float(NE), in1=iob, op0=ALU.mult, op1=ALU.add))
                dve.tensor_copy(rt[:, 960:960 + NE], bank(f"{L}.rank")[:, NT * NE:(NT + 1) * NE]).then_inc(emptied["dve"], 1)
                wait_emptied(dve, f"{L}.rank")
                for k in range(2):
                    line.link(dve.tensor_tensor(oh[k], oh[k], row, ALU.mult))
                    line.link(dve.tensor_reduce(small[:, 246:250], oh[k], AX.X, ALU.add))
                    ins = dve.tensor_copy(dest[:, k, :], small[:, 246:250])
                    if k == 0:
                        line.link(ins)
                    else:
                        ins.then_inc(routed, 1)
                NO = (NBLK - 1) * NE
                flag, pos = rt[:, 704:704 + NO], rt[:, 1024:1024 + NO]
                f3 = flag.rearrange("p (b e) -> p b e", b=NBLK - 1)
                line.link(dve.tensor_tensor(f3, rt[:, 960:960 + NE].unsqueeze(1).to_broadcast([P, NBLK - 1, NE]), thr[:], ALU.is_gt))
                line.link(dve.tensor_tensor_scan(pos, flag, flag, 0.0, ALU.add, ALU.max))
                if L:
                    dve.wait_ge(moe_done, L)
                line.link(dve.tensor_copy(ov_n[:], pos[0:1, NO - 1:NO]))
                line.link(dve.scalar_tensor_tensor(out=flag, in0=pos, scalar=place1[:, 0:1], in1=flag, op0=ALU.is_equal, op1=ALU.mult))
                for q, code in enumerate((code_e, code_r)):
                    line.link(dve.tensor_tensor(pos, flag, code[:].rearrange("p b e -> p (b e)"), ALU.mult))
                    line.link(dve.tensor_reduce(small[:, 246 + q:247 + q], pos, AX.X, ALU.add))
                if L:
                    dve.wait_ge(ov_stored, 16 * L)
                dve.tensor_copy(ov_code[:], small[:, 246:248]).then_inc(chosen, 1)

                def tokens_out(s_psum, val, s_sbuf):
                    dve.wait_ge(s_psum, val)
                    dve.tensor_tensor(tokT, ps[:, 0, :].rearrange("p (k n) -> p k n", k=KD),
                                      gains[:, 3 * L + 2, :].unsqueeze(2).to_broadcast([P, KD, CAP]), ALU.mult).then_inc(s_sbuf, 1)

                def hidden(c, s_):
                    dve.scalar_tensor_tensor(out=h_sb[0:CAP, :], in0=ps[CAP:P, 1, :], scalar=c[CAP:P, 1:2], in1=silu[CAP:P, :],
                                             op0=ALU.mult, op1=ALU.mult).then_inc(s_, 1)

                def one_hot(c, s_):
                    dve.tensor_scalar(onehot, iota_tok[:], c[:, 0:1], None, ALU.is_equal).then_inc(s_, 1)

                def split(q, n):
                    for h in range(2):
                        dve.wait_ge(q["y_high"], n * 2 + (1 + h))
                        dve.tensor_tensor(y_rest[HALF[1 - h], :], ps[HALF[h], 3, :], y_hm[h][HALF[h], :], ALU.subtract)\
                           .then_inc(q["y_rest"], 1)
                    for h in range(2):
                        dve.wait_ge(q["y_mid"], n * 2 + (1 + h))
                        o_ = HALF[1 - h]
                        dve.tensor_tensor(y_lo[o_, :], y_rest[o_, :], y_hm[h][o_, :], ALU.subtract).then_inc(q["y_low"], 1)

                def add_tile(t, s_):
                    b = 4 + 2 * (t % 2)
                    dve.tensor_tensor(x[:, t, :], ps[:, b:b + 2, :].rearrange("p a n -> p (a n)"), x[:, t, :], ALU.add).then_inc(s_, 1)

                def add_of(n, ts, started=True):
                    for t in ts:
                        dve.wait_ge(m["c_psum"], n * NT + (t + 1))
                        if started:
                            dve.wait_ge(m["c_added"], n * NT + (t - 3))
                        add_tile(t, m["c_added"])

                def expert(n, e, first=False, second=False):
                    dve.tensor_copy(cur[:], tabS[:, e, :] if isinstance(e, int) else
                                    tabS[:, bass.ds(e, 1), :].rearrange("p a b -> p (a b)")).then_inc(cur_ready, 1)
                    dve.wait_ge(cur_ready, n + 1)
                    dve.wait_ge(m["gu_psum"], n + 1)
                    dve.wait_ge(m["silu_done"], n + 1)
                    hidden(cur[:], m["h_done"])
                    if not first:
                        add_of(n + (-1), (0, 1), not second)
                    tokens_out(m["xt_psum"], n + (L + 2), m["xt_sbuf"])
                    if not first:
                        add_of(n + (-1), (2, 3), not second)
                    one_hot(cur[:], m["g_done"])
                    split(m, n)

                n0 = NE * L
                wait_emptied(dve, f"{L}.out.{NT - 1}.1")
                tokens_out(m["xt_psum"], n0 + (L + 1), m["xt_sbuf"])
                expert(n0, 0, first=True)
                expert(n0 + 1, 1, second=L == 0)
                with dve.Fori(2, NE) as e:
                    expert(e + n0, e)
                add_of(n0 + NE - 1, range(NT))
                o = ov[L]
                dve.wait_ge(ld["ovl"], 16 * (L + 1))
                n_ov = dve.value_load(ov_n[0:1, 0:1], min_val=0, max_val=OVMAX)
                dve.wait_ge(m["c_added"], NT * (n0 + NE))
                with dve.If(n_ov > 0):
                    with dve.Fori(0, n_ov) as i:
                        tokens_out(o["xt_psum"], i + 1, o["xt_sbuf"])
                        dve.wait_ge(o["cur"], i * 32 + 32)
                        one_hot(ov_cur[:, :], o["g_done"])
                        dve.wait_ge(o["gu_psum"], i + 1)
                        dve.wait_ge(o["silu_done"], i + 1)
                        hidden(ov_cur[:, :], o["h_done"])
                        split(o, i)
                        for t in range(NT):
                            dve.wait_ge(o["c_psum"], i * NT + (t + 1))
                            add_tile(t, o["c_added"])
                        wait_alone(dve, o["c_added"], i * NT + NT)
                dve.memset(small[:, 252:253], 0.0).then_inc(moe_done, 1)


_INS = ["x", "mem", "norm_mix", "norm_ffn", "mem_norm", "w_mem_kv", "xq_norm", "xk_norm", "w_out", "lru_w_in", "lru_conv_w",
        "lru_conv_b", "lru_w_a", "lru_b_a", "lru_w_x", "lru_b_x", "lru_lambda", "dsa_w_in", "dsa_q_norm", "dsa_k_norm",
        "dsa_w_uv", "rel_bias", "moe_w_group", "moe_b_group", "moe_w_router", "moe_b_router", "moe_w_gate", "moe_w_up",
        "moe_w_down"]


def kernel(**inputs):
    import concourse.bacc as bacc
    from concourse.bass_utils import run_bass_kernel_spmd

    nc = bacc.Bacc("TRN2", target_bir_lowering=False, num_devices=1)
    arrays, aps = {}, {}
    for name in _INS:
        v = np.ascontiguousarray(inputs[name])
        arrays[f"in_{name}"] = v
        aps[name] = nc.dram_tensor(f"in_{name}", v.shape, mybir.dt.from_np(v.dtype), kind="ExternalInput").ap()
    out = nc.dram_tensor("out", (1, S, D), F32, kind="ExternalOutput").ap()
    hybrid_trunk(nc, aps, out)
    r = run_bass_kernel_spmd(nc, [arrays], core_ids=[0])
    return r.results[0]["out"]
```

```python
from contextlib import ExitStack

import numpy as np

import concourse.bass as bass
from concourse import mybir

F32 = mybir.dt.float32
BF16 = mybir.dt.bfloat16
I32 = mybir.dt.int32
U32 = mybir.dt.uint32
ALU = mybir.AluOpType
ACT = mybir.ActivationFunctionType
AX = mybir.AxisListType

P = 128
D = 1024
KD = D // P
S = 512
NT = S // P
M = 256
EPS = 1e-6
XH, HD = 4, 64
XW = XH * HD
LRU = D - XW
NC = LRU // P
LB = LRU // 4
CONV = 4
HEADS = LRU // HD
VD = 128
TOPK = min(256, S // 4)
W0 = 2 * LRU + XW
IH = 4
C_Q, C_K, C_V = 0, LRU, LRU + HD
C_QI = C_V + VD
C_KI = C_QI + IH * HD
C_WI = C_KI + HD
C_XQ = C_WI + IH
W1 = C_XQ + XW
NB, MAXD = 32, 128
NG, EG = 4, 8
NE = NG * EG
FE = 512
KF = FE // P
CAP = 64
NBLK = S // CAP
OVMAX = 2 * S // CAP
NS = 3
R = NG + NE
BIG = -1.0e30
TAKEN = -3.0e38
NOTOK = 4096.0

R_CW, R_CB, R_BA, R_BX, R_LAM = 0, CONV * NC, (CONV + 1) * NC, (CONV + 2) * NC, (CONV + 3) * NC
R_XQ = (CONV + 4) * NC
NPRM = R_XQ + 6


def bucket_onehot():
    d = S - 1 - np.arange(S + P, dtype=np.int64)
    d = np.maximum(d, 0)
    df = np.maximum(d, 1).astype(np.float32)
    half = NB // 2
    large = half + (np.log(df / np.float32(half)) / np.float32(np.log(MAXD / half)) * np.float32(NB - half)).astype(np.int32)
    b = np.where(d < half, d, np.minimum(large, NB - 1))
    return (np.arange(NB)[:, None] == b[None, :]).astype(np.float32)


class Jobs:

    def __init__(self):
        self.number, self.reader, self.before = {}, [], []
        self.count = {"act": 0, "dve": 0}

    def add(self, name, reader):
        self.number[name] = len(self.reader)
        self.reader.append(reader)
        self.count[reader] += 1
        self.before.append(dict(self.count))

    def emptied(self, name):
        n = self.number[name]
        return self.reader[n], self.before[n][self.reader[n]]


def out_order():
    return [("out", 0), ("out", 1), ("fT", 0), ("out", 2), ("route", 0), ("fT", 1), ("out", 3), ("route", 1), ("fT", 2),
            ("route", 2), ("fT", 3), ("route", 3)]


MEMORY_AT = [(0,), (1, 2), (3,), ()]


def memory_products(L):
    return [f"{L}.memK.0", f"{L}.memK.1", f"{L}.memV.0", f"{L}.memV.1"]


def lru_order():
    steps = [("conv", c) for c in range(3)]
    for c in range(NC):
        steps += [("rec", c), ("conv", c + 3) if c < 3 else ("gate", c - 3)]
    return steps + [("gate", c) for c in range(NC - 3, NC)]


def attention_groups():
    return [(qb, g) for qb in range(NT) for g in range(HEADS // 4)]


def pt_reader(qb, g, s):
    return "act" if (s + g) % 2 else "dve"


def plan():
    j = Jobs()
    for L in range(2):
        if L == 0:
            for mt in range(2):
                for h in range(2):
                    j.add(f"memT.{mt}.{h}", "dve")
            for name in memory_products(0) + ["params", "bias0", "bias1"]:
                j.add(name, "act")
        for t in range(NT):
            for h in range(2):
                j.add(f"{L}.xT.{t}.{h}", "dve")
        if L == 0:
            j.add("0.sq.memK", "act")
            for what, c in lru_order():
                if what == "rec":
                    j.add(f"0.ra.{c}", "act")
                    j.add(f"0.rx.{c}", "act")
                elif what == "gate":
                    j.add(f"0.gate.{c}", "act")
                else:
                    j.add(f"0.xs.{c}", "act")
                    if c == 2:
                        for name in ("xq.0", "xq.1", "sq.xq.0", "sq.xq.1"):
                            j.add(f"0.{name}", "act")
        else:
            j.add("1.sq.memK", "act")
            j.add("1.ki", "act")
            j.add("1.qi.0", "act")
            j.add("1.sq.ki", "act")
            j.add("1.qi.1", "act")
            j.add("1.v.0", "act")
            j.add("1.v.1", "act")
            for qb in range(1, NT):
                for h in range(IH):
                    j.add(f"1.dot.{qb}.{h}", "act")
            last = None
            for name in ["k"] + [f"q.{c}" for c in range(NC)] + ["xq.0", "xq.1"]:
                j.add(f"1.{name}", "act")
                if last:
                    j.add(f"1.sq.{last}", "act")
                last = name
            j.add(f"1.sq.{last}", "act")
        for m in range(-2, NT):
            if m >= 0:
                j.add(f"{L}.xp.{m}.0", "act")
                j.add(f"{L}.xp.{m}.1", "dve")
            if m + 2 < NT:
                for par in range(2):
                    j.add(f"{L}.xl.{m + 2}.{par}", "act")
            if m >= 0:
                j.add(f"{L}.xo.{m}", "dve")
                if L == 0:
                    for i in MEMORY_AT[m]:
                        j.add(memory_products(1)[i], "act")
        if L == 1:
            gs = attention_groups()
            for m in range(-2, len(gs) + 1):
                if 0 <= m < len(gs):
                    qb, g = gs[m]
                    for s in range(qb + 1):
                        j.add(f"1.pt.{qb}.{g}.{s}", pt_reader(qb, g, s))
                if m >= 1:
                    qb, g = gs[m - 1]
                    j.add(f"1.uv.{qb}.{g}", "dve")
                if m + 2 < len(gs):
                    qb, g = gs[m + 2]
                    for h in range(4):
                        j.add(f"1.l.{qb}.{g}.{h}", "dve")
                if 0 <= m < len(gs):
                    qb, g = gs[m]
                    j.add(f"1.pv.{qb}.{g}", "act")
        for what, t in out_order():
            for h in range(2) if what != "route" else ():
                j.add(f"{L}.{what}.{t}.{h}", "dve")
            if what == "route":
                j.add(f"{L}.route.{t}", "dve")
        j.add(f"{L}.rank", "dve")
        j.add(f"{L}.table", "dve")
    return j


def hybrid_trunk(nc, a, out):
    jobs = plan()
    scratch_bias = nc.dram_tensor("scratch_bias", (HEADS, S + P), F32).ap()
    scratch_rep = nc.dram_tensor("scratch_rep", (P, HEADS, S + P), F32).ap()
    scratch_xn = [nc.dram_tensor(f"scratch_xn{L}", (S, D), F32).ap() for L in range(2)]
    scratch_tab = [nc.dram_tensor(f"scratch_tab{L}", (S * NE, 2), F32).ap() for L in range(2)]
    scratch_ov = nc.dram_tensor("scratch_ov", (2, OVMAX, 2), I32)
    onehot_dram = nc.inline_tensor(bucket_onehot(), name="bucket_onehot")

    with ExitStack() as ctx:
        def sb(name, shape, dt=F32):
            return ctx.enter_context(nc.sbuf_tensor(name, shape, dt))

        def sem(name):
            return ctx.enter_context(nc.semaphore(name))

        SLOT = 3 * KD * FE
        arena = sb("arena", [P, NS * SLOT])
        x = sb("x", [P, NT, D])
        xT = sb("xT", [P, KD, S])
        mix = sb("mix", [P, 8, S])
        xn = mix[:, :, :].rearrange("p a b -> p (a b)").rearrange("p (t d) -> p t d", t=NT)
        ident = sb("ident", [P, P])
        identb = sb("identb", [P, P], BF16)
        ones_head = sb("ones_head", [P, P])
        before = sb("before", [P, P], BF16)
        ones_b = sb("ones_b", [P, P], BF16)
        iota_tok = sb("iota_tok", [P, S])
        iota_e = sb("iota_e", [P, NE])
        thr = sb("thr", [P, NBLK - 1])
        rank_w = sb("rank_w", [P, NG])
        tokid = sb("tokid", [P, NT])
        place1 = sb("place1", [P, 1])
        prm = sb("prm", [P, NPRM])
        eps = sb("eps", [P, 1])
        gains = sb("gains", [P, 6, KD])
        w_route = sb("w_route", [P, KD, R])
        b_route = sb("b_route", [P, 2, R])
        memKT = sb("memKT", [P, 2, 2, M])
        memV = sb("memV", [P, 2, 2, XW])
        small = sb("small", [P, 256])
        soft = small[:, 16:64].rearrange("p (b c h) -> p b c h", b=3, c=4)
        choice = sb("choice", [P, NT, NE], BF16)
        dest = sb("dest", [P, 2, NT], I32)
        pay = sb("pay", [P, 2, NT, 2])
        tabS = sb("tabS", [P, NE + 1, 2])
        cur = sb("cur", [P, 2])
        idx = sb("idx", [CAP, NS], I32)
        ov_code = sb("ov_code", [P, 2], I32)
        ov_list = sb("ov_list", [1, 2 * OVMAX], I32)
        ov_n = sb("ov_n", [1, 1], I32)
        ov_cur = sb("ov_cur", [P, 2])
        ov_idx = sb("ov_idx", [CAP, 1], I32)
        ps = ctx.enter_context(nc.psum_tensor("ps", [P, 8, 512], F32))

        def area(at, *shape, dt=F32):
            n = int(np.prod(shape))
            words = n if dt == F32 else n // 2
            v = arena[:, at:at + words]
            if dt != F32:
                v = v.bitcast(dt)
            if len(shape) == 1:
                return v
            names = "abcd"[:len(shape)]
            return v.rearrange(f"p ({' '.join(names)}) -> p {' '.join(names)}", **dict(zip(names[1:], shape[1:])))

        w_out = area(NS * SLOT - KD * D, KD, D)
        start_area = area(NS * SLOT - KD * D, KD * D)
        w_in = [area(NS * SLOT - KD * D - KD * W0, KD, W0), area(2 * SLOT, KD, W1 - IH)]
        lo0 = NS * SLOT - KD * D - KD * W0
        w_kv = [area(0, KD, 2 * XW), area(NS * SLOT - KD * D - 6144, KD, 2 * XW)]
        mem = area(4096, 2, D)
        memT = [area(6144, KD, M), area(NS * SLOT - 2 * D, KD, M)]
        bucket_oh = start_area[0:NB, 0:S + P]
        bucket_bias = start_area[0:NB, 640:640 + HEADS]
        bias_rows = start_area[0:HEADS, 1024:1024 + S + P]
        prm_rows = start_area[0:NPRM, 2304:2304 + P]
        xs = area(8192, NC, S + CONV - 1)
        gate_w = area(11284, 2, 2, 3, LB)
        xc = area(0, NC, S)
        xqT = [area(3072, 2, S), area(5120, 2, S)]
        lru = area(4096, 2, 3, S)
        sqb = [area(7168, 2, S), area(6144, 2, S)]
        rsb = [area(4096, 2, S), area(7168, 2, S)]
        qT = area(0, NC, S)
        qiT = area(3072, 2, S)
        kT = area(4096, S)
        kiT = area(4608, S)
        T_all = area(8192, HEADS, S)
        v_sb = area(14336, NT, VD)
        w_uv = area(14848, HEADS, HD)
        wi_sb = area(15616, NT, IH)
        w_v = area(0, KD, VD + IH)
        masks = [area(15680 + 32 * q * (q + 1), (q + 1) * P, dt=BF16) for q in range(NT)]
        att = [lo0, 16320]
        xP_sb = [area(att[L], 3, XH, M) for L in range(2)]
        P_sb = area(att[1], 3, 4, S)
        PT_sb = [area(att[0] + 3 * XH * M, 2, 4, S), area(att[1] + 3 * 4 * S, 2, 4, S)]
        oT = area(att[1] + 5 * 4 * S, 2, 4 * P)
        relu = mix[:, 0:3, :]
        score = [None] + [mix[:, 2 + q, :] for q in range(1, NT)]
        xn_ffn = area(2 * SLOT, NT, D)
        slots = []
        for s in range(NS):
            slots.append((area(s * SLOT, KD, FE), area(s * SLOT + KD * FE, KD, FE), area(s * SLOT + 2 * KD * FE, KF, D)))
        flatT = xT[:, :, :].rearrange("p a b -> p (a b)")
        tokT = flatT[:, 0:512].rearrange("p (k n) -> p k n", k=KD)
        onehot = flatT[:, 512:768].bitcast(BF16)
        y_hm = [flatT[:, 768 + 256 * h:1024 + 256 * h].bitcast(BF16) for h in range(2)]
        y_lo = flatT[:, 1280:1536].bitcast(BF16)
        silu = flatT[:, 1536:2048]
        h_sb = flatT[:, 2048:2560]
        hT = flatT[:, 2560:2816].rearrange("p (j n) -> p j n", j=KF)
        flatM = mix[:, :, :].rearrange("p a b -> p (a b)")
        xg = [flatM[0:CAP, s * D:(s + 1) * D] for s in range(NS)]
        y_rest = flatM[:, NS * D:NS * D + 512]
        HALF = [slice(0, CAP), slice(CAP, P)]
        route_area = flatT[:, 2816:4096]
        place_hot = flatT[:, 512:1536].rearrange("p (k t c n) -> p k t c n", k=2, t=NT, c=2)
        expert_pay = flatT[:, 1536:2048].rearrange("p (k t c e) -> p k t c e", k=2, t=NT, c=2)
        pay_t = small[:, 64:80].rearrange("p (k t c) -> p k t c", k=2, t=NT)
        v8 = route_area[:, 928:960].rearrange("p (t n) -> p t n", t=NT)
        i8 = route_area[:, 1248:1280].bitcast(U32).rearrange("p (t n) -> p t n", t=NT)

        ld = {n: sem(f"ld_{n}") for n in ["mem", "x", "prm", "onehot", "gains", "broute", "wkv", "win", "winq", "wing", "wv", "wg",
                                          "wout", "wr", "bias", "wuv", "ovl"]}
        filled = sem("filled")
        emptied = {"act": sem("emptied_act"), "dve": sem("emptied_dve")}
        consts = sem("consts")
        act_line, dve_line, pool_line = sem("act_line"), sem("dve_line"), sem("pool_line")
        row_sums = sem("row_sums")
        rows_normed = sem("rows_normed")
        mem_spread = sem("mem_spread")
        sq_ready, root_ready = sem("sq_ready"), sem("root_ready")
        feat_normed = sem("feat_normed")
        gain_ready = sem("gain_ready")
        xc_ready = sem("xc_ready")
        lru_tanh = sem("lru_tanh")
        lru_log = sem("lru_log")
        lru_exp = sem("lru_exp")
        lru_sq = sem("lru_sq")
        lru_var = sem("lru_var")
        lru_h = sem("lru_h")
        lru_root = sem("lru_root")
        lru_y = sem("lru_y")
        lru_par_a, lru_par_d = sem("lru_par_a"), sem("lru_par_d")
        dots_used = sem("dots_used")
        causal = sem("causal")
        masked = sem("masked")
        x_max = sem("x_max")
        x_inv = sem("x_inv")
        x_prob = sem("x_prob")
        l_max = sem("l_max")
        l_exp = sem("l_exp")
        l_inv = sem("l_inv")
        l_prob = sem("l_prob")
        r_diff, r_exp = sem("r_diff"), sem("r_exp")
        chosen = sem("chosen")
        routed = sem("routed")
        xn_stored = sem("xn_stored")
        tab_zero = sem("tab_zero")
        scattered = sem("scattered")
        tab_ready = sem("tab_ready")
        placed = sem("placed")
        ov_stored = sem("ov_stored")
        bias_stored, bias_spread = sem("bias_stored"), sem("bias_spread")
        gu_landed = [sem(f"gu_landed{s}") for s in range(NS)]
        d_landed = [sem(f"d_landed{s}") for s in range(NS)]
        gathered = [sem(f"gathered{s}") for s in range(NS)]
        idx_ready, cur_ready = sem("idx_ready"), sem("cur_ready")
        names = ["xt_psum", "xt_sbuf", "gu_psum", "silu_done", "h_done", "ht_psum", "ht_sbuf", "y_psum", "y_high", "y_rest",
                 "y_mid", "y_low",
                 "g_done", "c_psum", "c_added"]
        m = {n: sem(n) for n in names}
        ov = [{n: sem(f"ov{L}_{n}") for n in names + ["landed", "cur", "idx", "gathered"]} for L in range(2)]
        moe_done = sem("moe_done")
        stored = sem("stored")

        def wait_alone(eng, s, value):
            eng.wait_ge(s, value)
            eng.nop(nofuse=True)

        def wait_filled(eng, name):
            eng.wait_ge(filled, jobs.number[name] + 1)

        def wait_emptied(eng, name):
            who, n = jobs.emptied(name)
            eng.wait_ge(emptied[who], n)

        def bank(name):
            return ps[:, jobs.number[name] % 8, :]

        class Line:

            def __init__(self, eng, s):
                self.eng, self.s, self.n = eng, s, 0

            def step(self, ins):
                ins.then_inc(self.s, 1)
                self.n += 1

            def settle(self):
                self.eng.wait_ge(self.s, self.n)

            def link(self, ins):
                self.step(ins)
                self.settle()

        rows = {}
        for L in range(2):
            for kind, n in (("mem", 2 - 2 * L), ("mix", NT), ("ffn", NT)):
                for t in range(n):
                    rows[L, kind, t] = len(rows) + 1
        feats = {}
        for f in ["0.memK", "0.xq.0", "0.xq.1", "1.memK", "1.ki", "1.k"] + [f"1.q.{c}" for c in range(NC)] + ["1.xq.0", "1.xq.1"]:
            feats[f] = len(feats) + 1

        by_log = ["1.k"] + [f"1.q.{c}" for c in range(NC)] + ["1.xq.0", "1.xq.1"]

        def rs_view(key):
            return rsb[int(key[0])][:, feats[key] % 2, :]

        slot_base = [[0, 0, 0], [11, 11, 10]]

        block = ctx.enter_context(nc.Block())

        @block.sync
        def _(sp):
            def expert_weights(L, e, s, before_):
                wg, wu, wd = slots[s]
                if before_ is not None:
                    sp.wait_ge(m["gu_psum"], before_)
                sp.dma_start(wg, a["moe_w_gate"][L, bass.ds(e, 1)].rearrange("a (p k) n -> p (a k) n", k=KD)).then_inc(gu_landed[s], 16)
                sp.dma_start(wu, a["moe_w_up"][L, bass.ds(e, 1)].rearrange("a (p k) n -> p (a k) n", k=KD)).then_inc(gu_landed[s], 16)
                if before_ is not None:
                    sp.wait_ge(m["y_psum"], before_)
                sp.dma_start(wd, a["moe_w_down"][L, bass.ds(e, 1)].rearrange("a (p j) n -> p (a j) n", j=KF)).then_inc(d_landed[s], 16)

            for L in range(2):
                if L == 0:
                    sp.dma_start(mem, a["mem"][0].rearrange("(t p) d -> p t d", p=P)).then_inc(ld["mem"], 16)
                    sp.dma_start(w_kv[0], a["w_mem_kv"][0].rearrange("(p k) n -> p k n", k=KD)).then_inc(ld["wkv"], 16)
                else:
                    sp.wait_ge(moe_done, L)
                if L == 0:
                    sp.dma_start(x[:], a["x"][0].rearrange("(t p) d -> p t d", p=P)).then_inc(ld["x"], 16)
                    sp.wait_ge(ld["broute"], 32)
                    w = a["lru_w_in"][0].rearrange("(p k) n -> p k n", k=KD)
                    for n, c0, c1 in (("win", 0, LRU), ("winq", 2 * LRU, W0), ("wing", LRU, 2 * LRU)):
                        sp.dma_start(w_in[0][:, :, c0:c1], w[:, :, c0:c1]).then_inc(ld[n], 16)
                if L == 0:
                    for g, src in enumerate((a["lru_w_a"][0], a["lru_w_x"][0])):
                        for pair in range(2):
                            even, odd = src[2 * pair], src[2 * pair + 1]
                            sp.dma_start(gate_w[:, g, pair, 0, :], even[0:128, :]).then_inc(ld["wg"], 16)
                            sp.dma_start(gate_w[0:64, g, pair, 1, :], even[128:LB, :]).then_inc(ld["wg"], 16)
                            sp.dma_start(gate_w[64:128, g, pair, 1, :], odd[0:64, :]).then_inc(ld["wg"], 16)
                            sp.dma_start(gate_w[:, g, pair, 2, :], odd[64:LB, :]).then_inc(ld["wg"], 16)
                else:
                    for n, c0, c1 in ((0, C_V, C_V + VD), (VD, C_WI, C_XQ)):
                        sp.dma_start(w_v[:, :, n:n + c1 - c0],
                                     a["dsa_w_in"][0].rearrange("(p k) n -> p k n", k=KD)[:, :, c0:c1]).then_inc(ld["wv"], 16)
                    sp.wait_ge(bias_spread, 16)
                    toeplitz = bass.AP(scratch_rep.tensor, P - 1, [[HEADS * (S + P) - 1, P], [S + P, HEADS], [1, S]])
                    sp.dma_start(T_all, toeplitz).then_inc(ld["bias"], 16)
                    sp.dma_start(w_uv, a["dsa_w_uv"][0].rearrange("h c d -> c h d")).then_inc(ld["wuv"], 16)
                if L == 0:
                    sp.wait_ge(tab_zero, 32)
                    sp.wait_ge(bias_stored, 16)
                    sp.dma_start(w_out[:, 0:6, :], a["w_out"][L].rearrange("(c p) n -> p c n", p=P)[:, 0:6, :]).then_inc(ld["wout"], 16)
                else:
                    wait_filled(sp, "1.xq.1")
                    sp.dma_start(w_out, a["w_out"][L].rearrange("(c p) n -> p c n", p=P)).then_inc(ld["wout"], 16)
                if L:
                    wait_filled(sp, "0.route.3")
                sp.dma_start(w_route[:, :, 0:NG], a["moe_w_group"][L].rearrange("(p k) n -> p k n", k=KD)).then_inc(ld["wr"], 16)
                sp.dma_start(w_route[:, :, NG:R], a["moe_w_router"][L].rearrange("(p k) n -> p k n", k=KD)).then_inc(ld["wr"], 16)
                if L == 0:
                    sp.wait_ge(bias_stored, 16)
                    sp.dma_start(scratch_rep, scratch_bias.unsqueeze(0).to_broadcast([P, HEADS, S + P])).then_inc(bias_spread, 16)
                    wait_filled(sp, f"0.gate.{NC - 1}")
                    sp.dma_start(w_kv[1], a["w_mem_kv"][1].rearrange("(p k) n -> p k n", k=KD)).then_inc(ld["wkv"], 16)
                    wait_filled(sp, "1.memV.1")
                    sp.dma_start(w_out[:, 6:8, :], a["w_out"][L].rearrange("(c p) n -> p c n", p=P)[:, 6:8, :]).then_inc(ld["wout"], 16)
                wait_filled(sp, f"{L}.out.0.0")
                expert_weights(L, 0, 0, None)
                expert_weights(L, 1, 1, None)
                for t in range(NT):
                    sp.wait_ge(rows_normed, rows[L, "ffn", t])
                    sp.dma_start(scratch_xn[L][t * P:(t + 1) * P, :], xn_ffn[:, t, :]).then_inc(xn_stored, 16)
                sp.wait_ge(xn_stored, 16 * NT * (L + 1))
                wait_filled(sp, f"{L}.fT.{NT - 1}.1")
                expert_weights(L, 2, 2, None)
                sp.wait_ge(chosen, 2 * L + 2)
                sp.dma_start(scratch_ov.ap()[L], ov_code[0:OVMAX, :]).then_inc(ov_stored, 16)
                with sp.Fori(0, (NE - 5) // 3) as i:
                    for j in range(3):
                        expert_weights(L, i * 3 + (3 + j), j, i * 3 + (NE * L + 1 + j))
                for e in (NE - 2, NE - 1):
                    expert_weights(L, e, e % NS, NE * L + e - 2)
                sp.wait_ge(ov_stored, 16 * (L + 1))
                sp.dma_start(ov_list[:], scratch_ov.ap()[L:L + 1].rearrange("a n c -> a (n c)")).then_inc(ld["ovl"], 16)
                o = ov[L]
                sp.wait_ge(ld["ovl"], 16 * (L + 1))
                if L == 0:
                    sp.wait_ge(m["y_psum"], NE - 2)
                    w = a["dsa_w_in"][0].rearrange("(p k) n -> p k n", k=KD)
                    sp.dma_start(w_in[1][:, :, 0:C_WI], w[:, :, 0:C_WI]).then_inc(ld["win"], 16)
                    sp.dma_start(w_in[1][:, :, C_WI:], w[:, :, C_XQ:]).then_inc(ld["win"], 16)
                n_ov = sp.value_load(ov_n[0:1, 0:1], min_val=0, max_val=OVMAX)
                with sp.If(n_ov > 0):
                    sp.wait_ge(scattered, 16 * 2 * NT * (L + 1))
                    sp.wait_ge(m["y_psum"], NE * (L + 1))
                    with sp.Fori(0, n_ov) as i:
                        e = sp.value_load(ov_list[0:1, bass.ds(i * 2, 1)], min_val=0, max_val=NE - 1)
                        r = sp.value_load(ov_list[0:1, bass.ds(i * 2 + 1, 1)], min_val=0, max_val=(NBLK - 1) * CAP * NE + NE - 1)
                        wg, wu, wd = slots[0]
                        sp.dma_start(wg, a["moe_w_gate"][L, bass.ds(e, 1)].rearrange("a (p k) n -> p (a k) n", k=KD)).then_inc(o["landed"], 16)
                        sp.dma_start(wu, a["moe_w_up"][L, bass.ds(e, 1)].rearrange("a (p k) n -> p (a k) n", k=KD)).then_inc(o["landed"], 16)
                        sp.dma_start(wd, a["moe_w_down"][L, bass.ds(e, 1)].rearrange("a (p j) n -> p (a j) n", j=KF)).then_inc(o["landed"], 16)
                        for h in range(2):
                            sp.dma_start(ov_cur[h * CAP:(h + 1) * CAP, :],
                                         scratch_tab[L][bass.ds(r, CAP, NE), :]).then_inc(o["cur"], 16)
                        wait_alone(sp, o["g_done"], i + 1)
                        wait_alone(sp, o["idx"], i + 1)
                        wait_alone(sp, o["y_psum"], i + 1)
            sp.wait_ge(scattered, 16 * 2 * NT * 2)
            sp.wait_ge(moe_done, 2)
            for t in range(NT):
                sp.dma_start(out[0, t * P:(t + 1) * P, :], x[:, t, :]).then_inc(stored, 16)
            sp.wait_ge(stored, 16 * NT)

        @block.gpsimd
        def _(pool):
            line = Line(pool, pool_line)
            for t_, val in ((ident, 0.0), (identb, 0.0), (before, 0.0), (ones_b, 1.0), (ones_head, 0.0)):
                line.step(pool.memset(t_[:], val))
            line.step(pool.memset(eps[:], EPS))
            line.step(pool.memset(tabS[:, NE, 0:1], NOTOK))
            line.step(pool.memset(tabS[:, NE, 1:2], 0.0))
            line.settle()
            for t_ in (ident, identb):
                line.step(pool.affine_select(out=t_[:], in_=t_[:], compare_op=ALU.not_equal, fill=1.0, base=0,
                                             pattern=[[-1, P]], channel_multiplier=1))
            line.step(pool.affine_select(out=before[:], in_=before[:], compare_op=ALU.is_ge, fill=1.0, base=0,
                                         pattern=[[-1, P]], channel_multiplier=1))
            for h in range(2):
                line.settle()
                line.link(pool.memset(ones_head[h * HD:(h + 1) * HD, h * HD:(h + 1) * HD], 1.0))
            line.step(pool.iota(iota_tok[:], pattern=[[1, S]], base=0, channel_multiplier=0, allow_small_or_imprecise_dtypes=True))
            line.step(pool.iota(iota_e[:], pattern=[[1, NE]], base=0, channel_multiplier=0, allow_small_or_imprecise_dtypes=True))
            line.step(pool.iota(thr[:], pattern=[[CAP, NBLK - 1]], base=CAP, channel_multiplier=0, allow_small_or_imprecise_dtypes=True))
            line.step(pool.iota(rank_w[:], pattern=[[-1, NG]], base=NG, channel_multiplier=0, allow_small_or_imprecise_dtypes=True))
            line.step(pool.iota(tokid[:], pattern=[[P, NT]], base=0, channel_multiplier=1, allow_small_or_imprecise_dtypes=True))
            line.step(pool.iota(place1[:], pattern=[[0, 1]], base=1, channel_multiplier=1, allow_small_or_imprecise_dtypes=True))
            empty = start_area[:, 2048:2048 + 2 * S * NE // P].rearrange("p (n c) -> p n c", c=2)
            line.step(pool.memset(empty[:, :, 0], NOTOK))
            line.step(pool.memset(empty[:, :, 1], 0.0))
            line.step(pool.memset(xs[:, :, 0:CONV - 1], 0.0))
            line.settle()
            line.step(pool.tensor_scalar(pay_t[:, :, :, 0], tokid[:].unsqueeze(1).to_broadcast([P, 2, NT]), -NOTOK, 1.0, ALU.add, ALU.mult))
            line.settle()
            pool.tensor_copy(pay[:, :, :, 0], tokid[:].unsqueeze(1).to_broadcast([P, 2, NT])).then_inc(consts, 1)
            for L in range(2):
                pool.dma_start(scratch_tab[L].rearrange("(p n) c -> p n c", p=P), empty).then_inc(tab_zero, 16)

            def scale_rows(buf, inv, n_heads, width):
                ins = None
                for h in range(n_heads):
                    ins = pool.tensor_scalar(buf[:, h, 0:width], buf[:, h, 0:width], inv[:, h:h + 1], 1.0, ALU.mult, ALU.mult)
                return ins

            def gather(L, e, s, n, first):
                if not first:
                    wait_alone(pool, m["xt_psum"], n - 2)
                pool.tensor_copy(idx[:, s:s + 1], tabS[0:CAP, e, 0:1] if isinstance(e, int) else
                                 tabS[0:CAP, bass.ds(e, 1), 0:1].rearrange("p a b -> p (a b)")).then_inc(idx_ready, 1)
                wait_alone(pool, idx_ready, n + 1)
                pool.indirect_dma_start(out=xg[s], out_offset=None, in_=scratch_xn[L],
                                        in_offset=bass.IndirectOffsetOnAxis(ap=idx[:, s:s + 1], axis=0),
                                        bounds_check=S - 1, oob_is_err=False).then_inc(gathered[s], 16)

            for L in range(2):
                if L == 1:
                    for qb in range(1, NT):
                        pool.wait_ge(dots_used, qb * IH)
                        d = score[qb][:, qb * P:(qb + 1) * P]
                        pool.affine_select(out=d, in_=d, compare_op=ALU.is_ge, fill=BIG, base=0,
                                           pattern=[[-1, P]], channel_multiplier=1).then_inc(causal, 1)
                        if qb == 1:
                            line.link(pool.memset(masks[0], 0.0))
                            pool.affine_select(out=masks[0][:, 0:P], in_=masks[0][:, 0:P], compare_op=ALU.is_ge, fill=BIG,
                                               base=0, pattern=[[-1, P]], channel_multiplier=1).then_inc(causal, 1)
                for t in range(NT):
                    pool.wait_ge(x_inv, L * NT + t + 1)
                    scale_rows(xP_sb[L][:, t % 3], soft[:, t % 3, 2, :], XH, M).then_inc(x_prob, 1)
                if L == 1:
                    for n, (qb, g) in enumerate(attention_groups()):
                        pool.wait_ge(l_inv, n + 1)
                        pool.wait_ge(l_exp, 4 * (n + 1))
                        scale_rows(P_sb[:, n % 3], soft[:, n % 3, 2, :], 4, (qb + 1) * P).then_inc(l_prob, 1)
                pool.wait_ge(tab_ready, L + 1)
                pool.wait_ge(xn_stored, 16 * NT * (L + 1))
                N = (NE + 1) * L
                for e in range(3):
                    if L and e == 0:
                        pool.wait_ge(moe_done, L)
                    gather(L, e, e, N + e, True)
                pool.wait_ge(tab_zero, 32)
                pool.wait_ge(routed, L + 1)
                for k in range(2):
                    for t in range(NT):
                        pool.indirect_dma_start(out=scratch_tab[L], out_offset=bass.IndirectOffsetOnAxis(ap=dest[:, k, t:t + 1], axis=0),
                                                in_=pay[:, k, t, :], in_offset=None).then_inc(scattered, 16)
                with pool.Fori(0, (NE + 1) // 3 - 1) as i:
                    for j in range(3):
                        gather(L, i * 3 + (3 + j), j, i * 3 + (N + 3 + j), False)
                o = ov[L]
                pool.wait_ge(ld["ovl"], 16 * (L + 1))
                n_ov = pool.value_load(ov_n[0:1, 0:1], min_val=0, max_val=OVMAX)
                with pool.If(n_ov > 0):
                    pool.wait_ge(m["xt_psum"], (NE + 1) * (L + 1))
                    with pool.Fori(0, n_ov) as i:
                        wait_alone(pool, o["cur"], i * 32 + 32)
                        pool.tensor_copy(ov_idx[:], ov_cur[0:CAP, 0:1]).then_inc(o["idx"], 1)
                        wait_alone(pool, o["idx"], i + 1)
                        pool.indirect_dma_start(out=xg[0], out_offset=None, in_=scratch_xn[L],
                                                in_offset=bass.IndirectOffsetOnAxis(ap=ov_idx[:], axis=0),
                                                bounds_check=S - 1, oob_is_err=False).then_inc(o["gathered"], 16)
                        wait_alone(pool, o["xt_psum"], i + 1)

        @block.scalar
        def _(act):
            line = Line(act, act_line)
            for n, name in enumerate(("mem_norm", "norm_mix", "norm_ffn")):
                act.dma_start(gains[:, n:6:3, :], a[name].rearrange("l (p k) -> p l k", k=KD)).then_inc(ld["gains"], 16)
            prm_src = ([(R_CW, CONV * NC, a["lru_conv_w"][0].rearrange("k (c p) -> (k c) p", p=P)),
                        (R_CB, NC, a["lru_conv_b"].rearrange("a (c p) -> (a c) p", p=P)),
                        (R_BA, NC, a["lru_b_a"].rearrange("a (c p) -> (a c) p", p=P)),
                        (R_BX, NC, a["lru_b_x"].rearrange("a (c p) -> (a c) p", p=P)),
                        (R_LAM, NC, a["lru_lambda"].rearrange("a (c p) -> (a c) p", p=P))])
            for r, n, src in prm_src:
                act.dma_start(prm_rows[r:r + n, :], src).then_inc(ld["prm"], 16)
            for n, src in enumerate((a["xq_norm"], a["xk_norm"])):
                for h in range(2):
                    act.dma_start(prm_rows[R_XQ + 2 * n:R_XQ + 2 * n + 2, h * HD:(h + 1) * HD], src).then_inc(ld["prm"], 16)
            for n, src in enumerate((a["dsa_q_norm"], a["dsa_k_norm"])):
                for h in range(2):
                    act.dma_start(prm_rows[R_XQ + 4 + n:R_XQ + 5 + n, h * HD:(h + 1) * HD], src).then_inc(ld["prm"], 16)
            act.dma_start(bucket_oh, onehot_dram.ap()).then_inc(ld["onehot"], 16)
            act.dma_start(bucket_bias, a["rel_bias"]).then_inc(ld["onehot"], 16)
            for n, name in enumerate(("moe_b_group", "moe_b_router")):
                c0, c1 = ((0, NG), (NG, R))[n]
                act.dma_start(b_route[:, :, c0:c1], a[name].unsqueeze(0).to_broadcast([P, 2, c1 - c0])).then_inc(ld["broute"], 16)
            act.wait_ge(consts, 1)

            def row_norm(L, kind, n, src, junk, ready):
                for t in range(n):
                    ready(t)
                    k = rows[L, kind, t]
                    c = small[:, k % 8:k % 8 + 1]
                    if k > 8:
                        act.wait_ge(rows_normed, k - 8)
                    line.link(act.activation(junk(t), src(t), ACT.Square, accum_out=c))
                    act.activation(c, c, ACT.Sqrt, bias=eps[:, 0:1], scale=1.0 / D).then_inc(row_sums, 1)

            def raw(L, name, dst, width=512):
                wait_filled(act, f"{L}.{name}")
                act.activation(dst, bank(f"{L}.{name}")[:, 0:width], ACT.Copy).then_inc(emptied["act"], 1)

            def squares(key, dst, jobs_read):
                n = feats[key]
                if n > 2:
                    k2 = [f for f, v in feats.items() if v == n - 2][0]
                    wait_filled(act, k2[0] + ".sq" + k2[1:])
                for jn in jobs_read:
                    wait_emptied(act, jn)
                act.activation(sqb[int(key[0])][:, n % 2, :], dst, ACT.Square).then_inc(sq_ready, 1)

            def roots(key):
                n = feats[key]
                jn = key[0] + ".sq" + key[1:]
                wait_filled(act, jn)
                if n > 2:
                    act.wait_ge(feat_normed, n - 2)
                if key in by_log:
                    act.activation(rs_view(key), bank(jn), ACT.Ln, bias=eps[:, 0:1], scale=1.0 / HD).then_inc(emptied["act"], 1)
                    wait_emptied(act, jn)
                    act.activation(rs_view(key), rs_view(key), ACT.Exp, scale=-0.5).then_inc(root_ready, 1)
                else:
                    act.activation(rs_view(key), bank(jn), ACT.Sqrt, bias=eps[:, 0:1], scale=1.0 / HD).then_inc(emptied["act"], 1)

            for L in range(2):
                def mem_ready(t):
                    if t == 0:
                        act.wait_ge(ld["mem"], 16 * (L + 1))

                def x_ready(t):
                    if t == 0:
                        act.wait_ge(ld["x"], 16)

                if L:
                    act.wait_ge(moe_done, L)
                else:
                    row_norm(L, "mem", 2, lambda t: mem[:, t, :], lambda t: xn[:, t, :], mem_ready)
                row_norm(L, "mix", NT, lambda t: x[:, t, :], lambda t: xn[:, t, :], x_ready)
                kraw = memKT[:, L, :, :].rearrange("p a b -> p (a b)")

                def memory_raw(ML, i):
                    if i < 2:
                        raw(ML, f"memK.{i}", memKT[:, ML, i, :], M)
                    else:
                        raw(ML, f"memV.{i - 2}", memV[:, ML, i - 2, :], XW)

                if L == 0:
                    for i in range(4):
                        memory_raw(0, i)
                squares(f"{L}.memK", kraw, [f"{L}.memK.1"])
                if L == 0:
                    wait_filled(act, "params")
                    act.activation(prm[:], bank("params")[:, 0:NPRM], ACT.Copy).then_inc(emptied["act"], 1)
                    for h in range(2):
                        wait_filled(act, f"bias{h}")
                        act.activation(bias_rows[:, h * 320:(h + 1) * 320], bank(f"bias{h}")[0:HEADS, 0:320], ACT.Copy).then_inc(emptied["act"], 1)
                    wait_emptied(act, "bias1")
                    act.dma_start(scratch_bias, bias_rows).then_inc(bias_stored, 16)
                    act.wait_ge(lru_par_d, 1)
                    act.activation(small[:, 112:112 + NC], small[:, 104:104 + NC], ACT.Exp).then_inc(lru_par_a, 1)
                    act.wait_ge(lru_par_d, 2)
                    act.activation(small[:, 128:128 + NC], small[:, 120:120 + NC], ACT.Ln).then_inc(lru_par_a, 1)
                roots(f"{L}.memK")
                if L == 0:
                    def conv_input(c):
                        wait_filled(act, f"0.xs.{c}")
                        act.activation(xs[:, c, CONV - 1:], bank(f"0.xs.{c}"), ACT.Copy).then_inc(emptied["act"], 1)

                    def recurrence(c):
                        b = lru[:, c % 2]
                        wait_filled(act, f"0.ra.{c}")
                        if c >= 2:
                            act.wait_ge(lru_h, c - 1)
                        if c == 0:
                            act.wait_ge(gain_ready, 1)
                            act.wait_ge(feat_normed, feats["0.xq.1"])
                        act.activation(b[:, 0, :], bank(f"0.ra.{c}"), ACT.Tanh, bias=small[:, 80 + c:81 + c], scale=0.5).then_inc(emptied["act"], 1)
                        wait_filled(act, f"0.rx.{c}")
                        act.activation(b[:, 2, :], bank(f"0.rx.{c}"), ACT.Tanh, bias=small[:, 86 + c:87 + c], scale=0.5).then_inc(emptied["act"], 1)
                        act.wait_ge(lru_log, c + 1)
                        act.activation(b[:, 1, :], b[:, 0, :], ACT.Tanh).then_inc(lru_tanh, 1)
                        act.wait_ge(lru_tanh, c + 1)
                        act.activation(b[:, 0, :], b[:, 0, :], ACT.Exp).then_inc(lru_exp, 1)
                        act.wait_ge(lru_exp, c + 1)
                        act.activation(xs[:, c, 0:S], b[:, 0, :], ACT.Square).then_inc(lru_sq, 1)
                        act.wait_ge(lru_var, c + 1)
                        act.activation(b[:, 1, :], b[:, 1, :], ACT.Sqrt, scale=-1.0).then_inc(lru_root, 1)

                    for what, c in lru_order():
                        if what == "rec":
                            recurrence(c)
                        elif what == "gate":
                            wait_filled(act, f"0.gate.{c}")
                            act.activation(mix[:, c, :], bank(f"0.gate.{c}"), ACT.Gelu_apprx_tanh).then_inc(emptied["act"], 1)
                        else:
                            conv_input(c)
                            if c == 2:
                                for q in range(2):
                                    raw(0, f"xq.{q}", xqT[0][:, q, :])
                                    squares(f"0.xq.{q}", xqT[0][:, q, :], [f"0.xq.{q}"])
                                for q in range(2):
                                    roots(f"0.xq.{q}")
                else:
                    raw(1, "ki", kiT)
                    squares("1.ki", kiT, ["1.ki"])
                    raw(1, "qi.0", qiT[:, 0, :])
                    roots("1.ki")
                    raw(1, "qi.1", qiT[:, 1, :])
                    for half in range(2):
                        wait_filled(act, f"1.v.{half}")
                        b = bank(f"1.v.{half}")[:, 0:2 * (VD + IH)].rearrange("p (t n) -> p t n", t=2)
                        act.activation(v_sb[:, 2 * half:2 * half + 2, :], b[:, :, 0:VD], ACT.Copy)
                        act.activation(wi_sb[:, 2 * half:2 * half + 2, :], b[:, :, VD:], ACT.Copy,
                                       scale=HD ** -0.5 * IH ** -0.5).then_inc(emptied["act"], 1)
                    for qb in range(1, NT):
                        n = (qb + 1) * P
                        for h in range(IH):
                            jn = f"1.dot.{qb}.{h}"
                            k = (qb - 1) * IH + h
                            wait_filled(act, jn)
                            if k >= 3:
                                act.wait_ge(dots_used, k - 2)
                            act.activation(relu[:, k % 3, 0:n], bank(jn)[:, 0:n], ACT.Relu).then_inc(emptied["act"], 1)
                    last = None
                    for name in ["k"] + [f"q.{c}" for c in range(NC)] + ["xq.0", "xq.1"]:
                        dst = kT if name == "k" else qT[:, int(name[2:]), :] if name[0] == "q" else xqT[1][:, int(name[3:]), :]
                        raw(1, name, dst)
                        squares(f"1.{name}", dst, [f"1.{name}"])
                        if last:
                            roots(f"1.{last}")
                        last = name
                    roots(f"1.{last}")
                for m_ in range(-2, NT):
                    if m_ >= 0:
                        jn = f"{L}.xp.{m_}.0"
                        wait_filled(act, jn)
                        if m_ >= 2:
                            wait_filled(act, f"{L}.xo.{m_ - 2}")
                        act.activation(PT_sb[L][:, m_ % 2, 0, :], bank(jn), ACT.Copy).then_inc(emptied["act"], 1)
                    t = m_ + 2
                    if t < NT:
                        b = xP_sb[L][:, t % 3]
                        if t >= 3:
                            wait_filled(act, f"{L}.xp.{t - 3}.1")
                        act.wait_ge(x_max, L * NT + t + 1)
                        for h in range(XH):
                            jn = f"{L}.xl.{t}.{h % 2}"
                            ins = act.activation(b[:, h, :], bank(jn)[:, (h // 2) * M:(h // 2 + 1) * M], ACT.Exp,
                                                 bias=soft[:, t % 3, 0, h:h + 1], accum_out=soft[:, t % 3, 1, h:h + 1])
                            if h >= 2:
                                ins.then_inc(emptied["act"], 1)
                    if L == 0 and m_ >= 0:
                        for i in MEMORY_AT[m_]:
                            memory_raw(1, i)
                if L == 1:
                    gs = attention_groups()
                    for m_ in range(-2, len(gs)):
                        if m_ >= 0:
                            qb, g = gs[m_]
                            for s in range(qb + 1):
                                if pt_reader(qb, g, s) == "act":
                                    jn = f"1.pt.{qb}.{g}.{s}"
                                    wait_filled(act, jn)
                                    act.activation(PT_sb[1][:, m_ % 2, s, :], bank(jn), ACT.Copy).then_inc(emptied["act"], 1)
                            jn = f"1.pv.{qb}.{g}"
                            wait_filled(act, jn)
                            act.activation(oT[:, m_ % 2, :], bank(jn), ACT.Copy).then_inc(emptied["act"], 1)
                        n = m_ + 2
                        if n < len(gs):
                            qb, g = gs[n]
                            act.wait_ge(l_max, n + 1)
                            for h in range(4):
                                b = P_sb[:, n % 3, h, 0:(qb + 1) * P]
                                act.activation(b, b, ACT.Exp, bias=soft[:, n % 3, 0, h:h + 1],
                                               accum_out=soft[:, n % 3, 1, h:h + 1]).then_inc(l_exp, 1)
                row_norm(L, "ffn", NT, lambda t: x[:, t, :], lambda t: xn_ffn[:, t, :],
                         lambda t: wait_emptied(act, f"{L}.out.{t}.1"))
                act.wait_ge(r_diff, 2 * L + 1)
                act.activation(small[:, 160:160 + NT * NG], small[:, 160:160 + NT * NG], ACT.Exp).then_inc(r_exp, 1)
                act.wait_ge(r_diff, 2 * L + 2)
                act.activation(small[:, 184:184 + NT], small[:, 184:184 + NT], ACT.Exp).then_inc(r_exp, 1)

                def split(q, n):
                    for h in range(2):
                        ins = act.activation(y_hm[h][HALF[h], :], ps[HALF[h], 3, :], ACT.Copy)
                        ins.then_inc(q["y_high"], 1)
                    for h in range(2):
                        act.wait_ge(q["y_rest"], n * 2 + (1 + h))
                        act.activation(y_hm[h][HALF[1 - h], :], y_rest[HALF[1 - h], :], ACT.Copy).then_inc(q["y_mid"], 1)

                def expert(n, first=False):
                    act.wait_ge(m["gu_psum"], n + 1)
                    act.activation(silu[CAP:2 * CAP, :], ps[0:CAP, 1, :], ACT.Silu).then_inc(m["silu_done"], 1)
                    act.wait_ge(m["ht_psum"], n + 1)
                    act.activation(hT, ps[:, 2, 0:KF * CAP].rearrange("p (j n) -> p j n", j=KF), ACT.Copy).then_inc(m["ht_sbuf"], 1)
                    act.wait_ge(m["y_psum"], n + 1)
                    if not first:
                        act.wait_ge(m["c_psum"], n * NT)
                    split(m, n)

                expert(NE * L, first=L == 0)
                with act.Fori(1, NE) as i:
                    expert(i + NE * L)
                o = ov[L]
                act.wait_ge(ld["ovl"], 16 * (L + 1))
                n_ov = act.value_load(ov_n[0:1, 0:1], min_val=0, max_val=OVMAX)
                with act.If(n_ov > 0):
                    act.wait_ge(m["c_psum"], NT * NE * (L + 1))
                    with act.Fori(0, n_ov) as i:
                        act.wait_ge(o["gu_psum"], i + 1)
                        act.activation(silu[CAP:2 * CAP, :], ps[0:CAP, 1, :], ACT.Silu).then_inc(o["silu_done"], 1)
                        act.wait_ge(o["ht_psum"], i + 1)
                        act.activation(hT, ps[:, 2, 0:KF * CAP].rearrange("p (j n) -> p j n", j=KF), ACT.Copy).then_inc(o["ht_sbuf"], 1)
                        act.wait_ge(o["y_psum"], i + 1)
                        split(o, i)

        @block.tensor
        def _(pe):
            state = {"n": 0}

            def open_bank(name):
                n = jobs.number[name]
                assert n == state["n"], (name, n, state)
                state["n"] += 1
                if n >= 8:
                    who = jobs.reader[n - 8]
                    pe.wait_ge(emptied[who], jobs.before[n - 8][who])
                return ps[:, n % 8, :]

            def product(name, pairs, cols=slice(0, 512), part=slice(0, P), close=True, b=None):
                b = open_bank(name) if b is None else b
                for i, (l, r) in enumerate(pairs):
                    ins = pe.matmul(b[part, cols], l, r, start=i == 0, stop=i == len(pairs) - 1)
                if close:
                    ins.then_inc(filled, 1)
                return b

            def transposes(name, src, parts=P, n=4, first=0, step=KD):
                b = open_bank(name)
                for k in range(n):
                    ins = pe.transpose(b[:, k * P:(k + 1) * P], src[:, first + k::step][:, 0:P], ident[:])
                ins.then_inc(filled, 1)

            def norm_sum(key):
                n = feats[key]
                pe.wait_ge(sq_ready, n)
                product(key[0] + ".sq" + key[1:], [(ones_head[:], sqb[int(key[0])][:, n % 2, :])])

            pe.wait_ge(consts, 1)
            for L in range(2):
                def memory_product(ML, i):
                    if i == 0:
                        pe.wait_ge(ld["wkv"], 16 * (ML + 1))
                    if i < 2:
                        product(f"{ML}.memK.{i}", [(w_kv[ML][:, k, i * P:(i + 1) * P], memT[ML][:, k, :]) for k in range(KD)],
                                cols=slice(0, M))
                    else:
                        product(f"{ML}.memV.{i - 2}", [(memT[ML][:, k, (i - 2) * P:(i - 1) * P], w_kv[ML][:, k, XW:2 * XW])
                                                       for k in range(KD)], cols=slice(0, XW))

                if L == 0:
                    for mt in range(2):
                        pe.wait_ge(rows_normed, rows[L, "mem", mt])
                        for h in range(2):
                            transposes(f"memT.{mt}.{h}", mem[:, mt, :], first=4 * h)
                    wait_emptied(pe, "memT.1.1")
                    for i in range(4):
                        memory_product(0, i)
                if L == 0:
                    pe.wait_ge(ld["prm"], 16 * 13)
                    b = open_bank("params")
                    pe.transpose(b[:, 0:NPRM], prm_rows[:, :], ident[0:NPRM, 0:NPRM]).then_inc(filled, 1)
                    pe.wait_ge(ld["onehot"], 32)
                    for h in range(2):
                        product(f"bias{h}", [(bucket_bias, bucket_oh[:, h * 320:(h + 1) * 320])],
                                cols=slice(0, 320), part=slice(0, HEADS))
                for t in range(NT):
                    pe.wait_ge(rows_normed, rows[L, "mix", t])
                    for h in range(2):
                        transposes(f"{L}.xT.{t}.{h}", xn[:, t, :], first=4 * h)
                norm_sum(f"{L}.memK")
                pe.wait_ge(ld["win"], 16 if L == 0 else 48)
                wait_emptied(pe, f"{L}.xT.{NT - 1}.1")

                def project(name, c0, width=P):
                    product(f"{L}.{name}", [(w_in[L][:, k, c0:c0 + width], xT[:, k, :]) for k in range(KD)])

                def project_twice(name, c0):
                    b = open_bank(f"{L}.{name}")
                    for k in range(KD):
                        for h in range(2):
                            ins = pe.matmul(b[h * HD:(h + 1) * HD, :], w_in[L][:, k, c0:c0 + HD], xT[:, k, :],
                                            start=k == 0, stop=k == KD - 1)
                    ins.then_inc(filled, 1)

                if L == 0:
                    def block_gates(c):
                        if c == 0:
                            pe.wait_ge(ld["wg"], 16 * 16)
                        pair, r = c // 3, c % 3
                        for g, nm in ((0, "ra"), (1, "rx")):
                            w = gate_w[:, g, pair]
                            x0, x1, x2 = (xc[:, 3 * pair + q, :] for q in range(3))
                            pe.wait_ge(xc_ready, 3 * pair + (2 if r == 0 else 3))
                            b = open_bank(f"0.{nm}.{c}")
                            if r == 0:
                                todo = [(slice(0, P), 0, slice(0, P))]
                            elif r == 1:
                                todo = [(slice(0, 64), 0, slice(P, LB)), (slice(64, P), 1, slice(0, 64))]
                            else:
                                todo = [(slice(0, P), 1, slice(64, LB))]
                            for part, odd, cols in todo:
                                if odd == 0:
                                    terms = [(w[:, 0, cols], x0), (w[0:64, 1, cols], x1[0:64])]
                                else:
                                    terms = [(w[64:P, 1, cols], x1[64:P]), (w[:, 2, cols], x2)]
                                for i, (l, rr) in enumerate(terms):
                                    ins = pe.matmul(b[part, :], l, rr, start=i == 0, stop=i == 1)
                            ins.then_inc(filled, 1)

                    for what, c in lru_order():
                        if what == "rec":
                            block_gates(c)
                        elif what == "gate":
                            if c == 0:
                                pe.wait_ge(ld["wing"], 16)
                            project(f"gate.{c}", LRU + c * P)
                        else:
                            project(f"xs.{c}", c * P)
                            if c == 2:
                                pe.wait_ge(ld["winq"], 16)
                                project("xq.0", 2 * LRU)
                                project("xq.1", 2 * LRU + P)
                                norm_sum("0.xq.0")
                                norm_sum("0.xq.1")
                else:
                    project_twice("ki", C_KI)
                    project("qi.0", C_QI)
                    norm_sum("1.ki")
                    project("qi.1", C_QI + P)
                    pe.wait_ge(ld["wv"], 32)
                    for half in range(2):
                        b = open_bank(f"1.v.{half}")
                        for tt in range(2):
                            t = 2 * half + tt
                            for k in range(KD):
                                ins = pe.matmul(b[:, tt * (VD + IH):(tt + 1) * (VD + IH)], xT[:, k, t * P:(t + 1) * P], w_v[:, k, :],
                                                start=k == 0, stop=k == KD - 1)
                        ins.then_inc(filled, 1)
                    wait_emptied(pe, "1.qi.1")
                    pe.wait_ge(feat_normed, feats["1.ki"])
                    for qb in range(1, NT):
                        for h in range(IH):
                            r0 = slice((h % 2) * HD, (h % 2) * HD + HD)
                            product(f"1.dot.{qb}.{h}", [(qiT[r0, h // 2, qb * P:(qb + 1) * P], kiT[r0, 0:(qb + 1) * P])],
                                    cols=slice(0, (qb + 1) * P))
                    last = None
                    for name, c0 in [("k", C_K)] + [(f"q.{c}", C_Q + c * P) for c in range(NC)] + [("xq.0", C_WI), ("xq.1", C_WI + P)]:
                        if name == "k":
                            project_twice("k", C_K)
                        else:
                            project(name, c0)
                        if last:
                            norm_sum(f"1.{last}")
                        last = name
                    norm_sum(f"1.{last}")

                for m_ in range(-2, NT):
                    if m_ >= 0:
                        pe.wait_ge(x_prob, L * NT + m_ + 1)
                        for mt in range(2):
                            b = open_bank(f"{L}.xp.{m_}.{mt}")
                            for h in range(XH):
                                ins = pe.transpose(b[:, h * P:(h + 1) * P], xP_sb[L][:, m_ % 3, h, mt * P:(mt + 1) * P], ident[:])
                            ins.then_inc(filled, 1)
                    t = m_ + 2
                    if t < NT:
                        if t == 0:
                            pe.wait_ge(feat_normed, feats[f"{L}.xq.1"])
                        bs = [open_bank(f"{L}.xl.{t}.{par}") for par in range(2)]
                        for h in range(XH):
                            r0 = slice((h % 2) * HD, (h % 2) * HD + HD)
                            ins = pe.matmul(bs[h % 2][:, (h // 2) * M:(h // 2 + 1) * M], xqT[L][r0, h // 2, t * P:(t + 1) * P],
                                            memKT[r0, L, h // 2, :], start=True, stop=True)
                            if h >= 2:
                                ins.then_inc(filled, 1)
                    if m_ >= 0:
                        b = open_bank(f"{L}.xo.{m_}")
                        wait_emptied(pe, f"{L}.xp.{m_}.0")
                        wait_emptied(pe, f"{L}.xp.{m_}.1")
                        for h in range(XH):
                            for mt in range(2):
                                ins = pe.matmul(b[(h % 2) * HD:(h % 2) * HD + HD, (h // 2) * P:(h // 2 + 1) * P],
                                                memV[:, L, mt, h * HD:(h + 1) * HD], PT_sb[L][:, m_ % 2, mt, h * P:(h + 1) * P],
                                                start=mt == 0, stop=mt == 1)
                        ins.then_inc(filled, 1)
                        if L == 0:
                            for i in MEMORY_AT[m_]:
                                memory_product(1, i)
                if L == 1:
                    gs = attention_groups()
                    for m_ in range(-2, len(gs) + 1):
                        if 0 <= m_ < len(gs):
                            qb, g = gs[m_]
                            pe.wait_ge(l_prob, m_ + 1)
                            for s in range(qb + 1):
                                b = open_bank(f"1.pt.{qb}.{g}.{s}")
                                for h in range(4):
                                    ins = pe.transpose(b[:, h * P:(h + 1) * P], P_sb[:, m_ % 3, h, s * P:(s + 1) * P], ident[:])
                                ins.then_inc(filled, 1)
                        if m_ >= 1:
                            qb, g = gs[m_ - 1]
                            b = open_bank(f"1.uv.{qb}.{g}")
                            wait_emptied(pe, f"1.pv.{qb}.{g}")
                            if m_ == 1:
                                pe.wait_ge(ld["wuv"], 16)
                            for h in range(4):
                                hh = 4 * g + h
                                ins = pe.matmul(b[(hh % 2) * HD:(hh % 2) * HD + HD, (h // 2) * P:(h // 2 + 1) * P],
                                                w_uv[:, hh, :], oT[:, (m_ - 1) % 2, h * P:(h + 1) * P], start=True, stop=True)
                            ins.then_inc(filled, 1)
                        n = m_ + 2
                        if n < len(gs):
                            qb, g = gs[n]
                            w = (qb + 1) * P
                            if g == 0:
                                if qb == 0:
                                    pe.wait_ge(causal, 2)
                                else:
                                    pe.wait_ge(masked, qb)
                            bs = [open_bank(f"1.l.{qb}.{g}.{h}") for h in range(4)]
                            for h in range(4):
                                pe.matmul(bs[h][:, 0:w], identb[:], masks[qb][:, 0:w], start=True, stop=False)
                            for h in range(4):
                                hh = 4 * g + h
                                r0 = slice((hh % 2) * HD, (hh % 2) * HD + HD)
                                pe.matmul(bs[h][:, 0:w], qT[r0, hh // 2, qb * P:(qb + 1) * P], kT[r0, 0:w],
                                          start=False, stop=True).then_inc(filled, 1)
                        if 0 <= m_ < len(gs):
                            qb, g = gs[m_]
                            b = open_bank(f"1.pv.{qb}.{g}")
                            for s in range(qb + 1):
                                wait_emptied(pe, f"1.pt.{qb}.{g}.{s}")
                                ins = pe.matmul(b, v_sb[:, s, :], PT_sb[1][:, m_ % 2, s, :], start=s == 0, stop=s == qb)
                            ins.then_inc(filled, 1)
                pe.wait_ge(ld["wout"], 32 + 16 * L)
                wait_emptied(pe, f"{L}.xo.{NT - 1}")
                if L == 0:
                    pe.wait_ge(lru_y, NC)
                else:
                    wait_emptied(pe, f"1.uv.{NT - 1}.{HEADS // 4 - 1}")
                for what, t in out_order():
                    if what == "out":
                        for h in range(2):
                            product(f"{L}.out.{t}.{h}", [(mix[:, c, t * P:(t + 1) * P], w_out[:, c, h * 512:(h + 1) * 512]) for c in range(8)])
                    elif what == "fT":
                        pe.wait_ge(rows_normed, rows[L, "ffn", t])
                        for h in range(2):
                            transposes(f"{L}.fT.{t}.{h}", xn_ffn[:, t, :], first=4 * h)
                    else:
                        if t == 0:
                            pe.wait_ge(ld["wr"], 32 * (L + 1))
                        wait_emptied(pe, f"{L}.fT.{t}.1")
                        product(f"{L}.route.{t}", [(xT[:, k, t * P:(t + 1) * P], w_route[:, k, :]) for k in range(KD)], cols=slice(0, R))
                b = open_bank(f"{L}.rank")
                pe.wait_ge(chosen, 2 * L + 1)
                for t in range(NT):
                    for u in range(t + 1):
                        pe.matmul(b[:, t * NE:(t + 1) * NE], before[:] if u == t else ones_b[:], choice[:, u, :],
                                  start=u == 0, stop=u == t)
                for u in range(NT):
                    ins = pe.matmul(b[:, NT * NE:(NT + 1) * NE], ones_b[:], choice[:, u, :], start=u == 0, stop=u == NT - 1)
                ins.then_inc(filled, 1)
                b = open_bank(f"{L}.table")
                pe.wait_ge(placed, L + 1)
                for k in range(2):
                    for t in range(NT):
                        ins = pe.matmul(b[:, 0:2 * NE], place_hot[:, k, t].rearrange("p c n -> p (c n)"),
                                        expert_pay[:, k, t].rearrange("p c e -> p (c e)"), start=k + t == 0, stop=k + t == NT)
                ins.then_inc(filled, 1)
                for n in range(state["n"] - 8, state["n"]):
                    who = jobs.reader[n]
                    pe.wait_ge(emptied[who], jobs.before[n][who])

                def tokens_T(src, s_):
                    for k in range(KD):
                        ins = pe.transpose(ps[:, 0, k * CAP:(k + 1) * CAP], src[:, k::KD][:, 0:P], ident[0:CAP, 0:CAP])
                    ins.then_inc(s_, 1)

                def gate_up(slot, s_):
                    wg, wu, _ = slots[slot]
                    for k in range(KD):
                        pe.matmul(ps[0:CAP, 1, :], tokT[:, k, :], wg[:, k, :], start=k == 0, stop=k == KD - 1)
                        ins = pe.matmul(ps[CAP:P, 1, :], tokT[:, k, :], wu[:, k, :], start=k == 0, stop=k == KD - 1)
                    ins.then_inc(s_, 1)

                def hidden_T(s_):
                    for j in range(KF):
                        ins = pe.transpose(ps[:, 2, j * CAP:(j + 1) * CAP], h_sb[0:CAP, j::KF][:, 0:P], ident[0:CAP, 0:CAP])
                    ins.then_inc(s_, 1)

                def down(slot, s_):
                    wd = slots[slot][2]
                    for j in range(KF):
                        pe.matmul(ps[0:CAP, 3, :], hT[:, j, :], wd[:, j, 0:512], start=j == 0, stop=j == KF - 1)
                        ins = pe.matmul(ps[CAP:P, 3, :], hT[:, j, :], wd[:, j, 512:D], start=j == 0, stop=j == KF - 1)
                    ins.then_inc(s_, 1)

                def combine(t, s_):
                    for h in range(2):
                        b = ps[:, 4 + 2 * (t % 2) + h, :]
                        lo = HALF[1 - h]
                        pe.matmul(b, onehot[:, t * P:(t + 1) * P], y_hm[h], start=True, stop=False)
                        ins = pe.matmul(b, onehot[lo, t * P:(t + 1) * P], y_lo[lo, :], start=False, stop=True)
                    ins.then_inc(s_, 1)

                def combine_of(n, ts, started=True):
                    for t in ts:
                        if t == 0:
                            pe.wait_ge(m["y_mid"], n * 2 + 2)
                            pe.wait_ge(m["y_low"], n * 2 + 2)
                            pe.wait_ge(m["g_done"], n + 1)
                        if started or t >= 2:
                            pe.wait_ge(m["c_added"], n * NT + (t - 1))
                        combine(t, m["c_psum"])

                def expert(n, slot, landed, gath, first=False, second=False):
                    pe.wait_ge(gu_landed[slot], landed * 32)
                    pe.wait_ge(m["xt_sbuf"], n + (L + 1))
                    gate_up(slot, m["gu_psum"])
                    if not first:
                        combine_of(n + (-1), (0, 1), not second)
                    wait_alone(pe, m["h_done"], n + 1)
                    hidden_T(m["ht_psum"])
                    wait_alone(pe, gathered[(slot + 1) % NS], gath * 16)
                    tokens_T(xg[(slot + 1) % NS], m["xt_psum"])
                    pe.wait_ge(m["ht_sbuf"], n + 1)
                    pe.wait_ge(d_landed[slot], landed * 16)
                    down(slot, m["y_psum"])
                    if not first:
                        combine_of(n + (-1), (2, 3))

                base = slot_base[L]
                gb = 11 * L
                n0 = NE * L
                pe.wait_ge(gathered[0], 16 * (gb + 1))
                tokens_T(xg[0], m["xt_psum"])
                expert(n0, 0, base[0] + 1, gb + 1, first=True)
                expert(n0 + 1, 1, base[1] + 1, gb + 1, second=L == 0)
                with pe.Fori(0, (NE - 2) // 3) as i:
                    expert(i * 3 + (n0 + 2), 2, i + (base[2] + 1), i + (gb + 2))
                    expert(i * 3 + (n0 + 3), 0, i + (base[0] + 2), i + (gb + 2))
                    expert(i * 3 + (n0 + 4), 1, i + (base[1] + 2), i + (gb + 2))
                combine_of(n0 + NE - 1, (0, 1, 2, 3))
                o = ov[L]
                pe.wait_ge(ld["ovl"], 16 * (L + 1))
                n_ov = pe.value_load(ov_n[0:1, 0:1], min_val=0, max_val=OVMAX)
                with pe.If(n_ov > 0):
                    pe.wait_ge(m["c_added"], NT * (n0 + NE))
                    pe.wait_ge(m["xt_sbuf"], (NE + 1) * (L + 1))
                    with pe.Fori(0, n_ov) as i:
                        wait_alone(pe, o["gathered"], i * 16 + 16)
                        tokens_T(xg[0], o["xt_psum"])
                        pe.wait_ge(o["xt_sbuf"], i + 1)
                        pe.wait_ge(o["landed"], i * 48 + 48)
                        gate_up(0, o["gu_psum"])
                        wait_alone(pe, o["h_done"], i + 1)
                        hidden_T(o["ht_psum"])
                        pe.wait_ge(o["ht_sbuf"], i + 1)
                        down(0, o["y_psum"])
                        pe.wait_ge(o["y_mid"], i * 2 + 2)
                        pe.wait_ge(o["y_low"], i * 2 + 2)
                        pe.wait_ge(o["g_done"], i + 1)
                        for t in range(NT):
                            if t >= 2:
                                pe.wait_ge(o["c_added"], i * NT + (t - 1))
                            combine(t, o["c_psum"])
                        wait_alone(pe, o["c_added"], i * NT + NT)
                pe.wait_ge(moe_done, L + 1)

        @block.vector
        def _(dve):
            line = Line(dve, dve_line)

            def rows_normalise(L, kind, ts, src, dst, ready=lambda t: None):
                for t in ts:
                    k = rows[L, kind, t]
                    c = small[:, k % 8:k % 8 + 1]
                    r = small[:, 8 + k % 8:9 + k % 8]
                    dve.wait_ge(row_sums, k)
                    ready(t)
                    line.link(dve.reciprocal(r, c))
                    dve.tensor_scalar(dst(t), src(t), r, None, ALU.mult).then_inc(rows_normed, 1)
                    dve.wait_ge(rows_normed, k)

            def features_normalise(key, dst, gain):
                n = feats[key]
                r = rs_view(key)
                if key in by_log:
                    dve.wait_ge(root_ready, by_log.index(key) + 1)
                else:
                    wait_emptied(dve, key[0] + ".sq" + key[1:])
                    line.link(dve.reciprocal(r, r))
                dve.scalar_tensor_tensor(out=dst, in0=dst, scalar=gain, in1=r, op0=ALU.mult, op1=ALU.mult).then_inc(feat_normed, 1)

            def spread_gain(name, dst, g, h, width, last=True):
                wait_filled(dve, name)
                ins = dve.tensor_tensor(dst, bank(name).rearrange("p (k n) -> p k n", k=4)[:, :, 0:width],
                                        gains[:, g, 4 * h:4 * h + 4].unsqueeze(2).to_broadcast([P, 4, width]), ALU.mult)
                ins.then_inc(emptied["dve"] if last else mem_spread, 1)

            one = small[:, 155:156]
            dve.wait_ge(consts, 1)

            for L in range(2):
                if L == 0:
                    rows_normalise(L, "mem", range(2), lambda t: mem[:, t, :], lambda t: mem[:, t, :])
                    dve.wait_ge(ld["gains"], 48)
                    for mt in range(2):
                        for h in range(2):
                            for ML in (1, 0):
                                spread_gain(f"memT.{mt}.{h}", memT[ML][:, 4 * h:4 * h + 4, mt * P:(mt + 1) * P], 3 * ML, h, P, ML == 0)
                rows_normalise(L, "mix", range(NT), lambda t: x[:, t, :], lambda t: xn[:, t, :])
                for t in range(NT):
                    for h in range(2):
                        spread_gain(f"{L}.xT.{t}.{h}", xT[:, 4 * h:4 * h + 4, t * P:(t + 1) * P], 3 * L + 1, h, P)
                if L == 0:
                    wait_emptied(dve, "params")
                    lam = prm[:, R_LAM:R_LAM + NC]
                    line.link(dve.tensor_scalar(small[:, 104:104 + NC], lam, -1.0, None, ALU.mult))
                    line.link(dve.tensor_tensor(small[:, 96:96 + NC], small[:, 104:104 + NC], lam, ALU.max))
                    dve.tensor_scalar(small[:, 104:104 + NC], small[:, 96:96 + NC], -1.0, None, ALU.mult).then_inc(lru_par_d, 1)
                    dve.wait_ge(lru_par_a, 1)
                    dve.tensor_scalar(small[:, 120:120 + NC], small[:, 112:112 + NC], 1.0, None, ALU.add).then_inc(lru_par_d, 1)
                    dve.wait_ge(lru_par_d, 2)
                    line.link(dve.tensor_scalar(small[:, 96:96 + NC], small[:, 120:120 + NC], -1.0, None, ALU.add))
                    line.link(dve.tensor_scalar(small[:, 136:136 + NC], small[:, 96:96 + NC], 0.0, None, ALU.is_equal))
                    line.link(dve.tensor_tensor(small[:, 96:96 + NC], small[:, 96:96 + NC], small[:, 136:136 + NC], ALU.add))
                    line.link(dve.reciprocal(small[:, 96:96 + NC], small[:, 96:96 + NC]))
                    dve.wait_ge(lru_par_a, 2)
                    line.link(dve.tensor_tensor(small[:, 136:136 + NC], small[:, 136:136 + NC], small[:, 128:128 + NC], ALU.add))
                    line.link(dve.tensor_tensor(small[:, 136:136 + NC], small[:, 136:136 + NC], small[:, 96:96 + NC], ALU.mult))
                    line.link(dve.tensor_tensor(small[:, 136:136 + NC], small[:, 136:136 + NC], small[:, 112:112 + NC], ALU.mult))
                    line.link(dve.tensor_scalar(small[:, 96:96 + NC], lam, -1.0, 0.0, ALU.mult, ALU.max))
                    line.link(dve.tensor_tensor(small[:, 136:136 + NC], small[:, 136:136 + NC], small[:, 96:96 + NC], ALU.add))
                    line.link(dve.tensor_scalar(small[:, 144:144 + NC], small[:, 136:136 + NC], -4.0, None, ALU.mult))
                    line.link(dve.tensor_scalar(prm[:, R_BA:R_BA + 2 * NC], prm[:, R_BA:R_BA + 2 * NC], 0.5, None, ALU.mult))
                    line.link(dve.tensor_copy(small[:, 80:80 + 2 * NC], prm[:, R_BA:R_BA + 2 * NC]))
                    for n, (g0, g1) in enumerate(((R_XQ, R_XQ + 2), (R_XQ + 1, R_XQ + 3), (R_XQ + 4, R_XQ + 5))):
                        line.step(dve.scalar_tensor_tensor(out=small[:, 152 + n:153 + n], in0=prm[:, g0:g0 + 1], scalar=0.125,
                                                           in1=prm[:, g1:g1 + 1], op0=ALU.mult, op1=ALU.mult))
                    line.settle()
                    dve.memset(small[:, 155:156], 1.0).then_inc(gain_ready, 1)
                    dve.wait_ge(gain_ready, 1)
                    dve.wait_ge(ld["broute"], 32)
                features_normalise(f"{L}.memK", memKT[:, L, :, :].rearrange("p a b -> p (a b)"), small[:, 152 + L:153 + L])
                if L == 0:
                    def convolve(c):
                        wait_emptied(dve, f"0.xs.{c}")
                        line.link(dve.tensor_scalar(xc[:, c, :], xs[:, c, 0:S], prm[:, R_CW + c:R_CW + c + 1],
                                                    prm[:, R_CB + c:R_CB + c + 1], ALU.mult, ALU.add))
                        for k in range(1, CONV):
                            r = R_CW + k * NC + c
                            ins = dve.scalar_tensor_tensor(out=xc[:, c, :], in0=xs[:, c, k:k + S], scalar=prm[:, r:r + 1],
                                                           in1=xc[:, c, :], op0=ALU.mult, op1=ALU.add)
                            if k < CONV - 1:
                                line.link(ins)
                            else:
                                ins.then_inc(xc_ready, 1)
                    def recurrence(c):
                        b = lru[:, c % 2]
                        wait_emptied(dve, f"0.rx.{c}")
                        dve.tensor_scalar(b[:, 0, :], b[:, 0, :], 1.0, small[:, 144 + c:145 + c], ALU.add, ALU.mult).then_inc(lru_log, 1)
                        dve.wait_ge(xc_ready, c + 1)
                        line.step(dve.scalar_tensor_tensor(out=b[:, 2, :], in0=b[:, 2, :], scalar=1.0, in1=xc[:, c, :],
                                                           op0=ALU.add, op1=ALU.mult))
                        dve.wait_ge(lru_sq, c + 1)
                        d = xs[:, c, 0:S]
                        dve.scalar_tensor_tensor(out=b[:, 1, :], in0=d, scalar=1.0, in1=b[:, 1, :], op0=ALU.add, op1=ALU.mult)\
                           .then_inc(lru_var, 1)
                        dve.wait_ge(lru_root, c + 1)
                        line.link(dve.scalar_tensor_tensor(out=b[:, 1, :], in0=b[:, 1, :], scalar=0.5, in1=b[:, 2, :],
                                                           op0=ALU.mult, op1=ALU.mult))
                        dve.tensor_tensor_scan(d, b[:, 0, :], b[:, 1, :], 0.0, ALU.mult, ALU.add).then_inc(lru_h, 1)

                    for what, c in lru_order():
                        if what == "conv":
                            convolve(c)
                            if c == 2:
                                for q in range(2):
                                    features_normalise(f"0.xq.{q}", xqT[0][:, q, :], one)
                        elif what == "rec":
                            recurrence(c)
                    for c in range(NC):
                        dve.wait_ge(lru_h, c + 1)
                        wait_emptied(dve, f"0.gate.{c}")
                        dve.tensor_tensor(mix[:, c, :], mix[:, c, :], xs[:, c, 0:S], ALU.mult).then_inc(lru_y, 1)
                else:
                    features_normalise("1.ki", kiT, one)

                    def scores(qb):
                        n = (qb + 1) * P
                        for h in range(IH):
                            k = (qb - 1) * IH + h
                            wait_emptied(dve, f"1.dot.{qb}.{h}")
                            if h == 0:
                                dve.tensor_scalar(score[qb][:, 0:n], relu[:, k % 3, 0:n], wi_sb[:, qb, 0:1], None, ALU.mult).then_inc(dots_used, 1)
                            else:
                                dve.wait_ge(dots_used, k)
                                dve.scalar_tensor_tensor(out=score[qb][:, 0:n], in0=relu[:, k % 3, 0:n], scalar=wi_sb[:, qb, h:h + 1],
                                                         in1=score[qb][:, 0:n], op0=ALU.mult, op1=ALU.add).then_inc(dots_used, 1)

                    def take_largest(qb):
                        n = (qb + 1) * P
                        dve.wait_ge(causal, qb if qb == 1 else qb + 1)
                        for r in range(TOPK // 8):
                            line.link(dve.max(small[:, 200:208], score[qb][:, 0:n]))
                            line.link(dve.match_replace(score[qb][:, 0:n], small[:, 200:208], score[qb][:, 0:n], TAKEN))
                        dve.tensor_scalar(masks[qb][:, 0:n], score[qb][:, 0:n], TAKEN / 1.5, BIG, ALU.is_gt, ALU.mult).then_inc(masked, 1)

                    for qb in range(1, NT):
                        scores(qb)
                    take_largest(1)
                    features_normalise("1.k", kT, small[:, 154:155])
                    features_normalise("1.q.0", qT[:, 0, :], one)
                    take_largest(2)
                    for c in range(1, 4):
                        features_normalise(f"1.q.{c}", qT[:, c, :], one)
                    take_largest(3)
                    for c in range(4, NC):
                        features_normalise(f"1.q.{c}", qT[:, c, :], one)
                    for c in range(2):
                        features_normalise(f"1.xq.{c}", xqT[1][:, c, :], one)
                for m_ in range(-2, NT):
                    if m_ >= 0:
                        jn = f"{L}.xp.{m_}.1"
                        wait_filled(dve, jn)
                        if m_ >= 2:
                            wait_filled(dve, f"{L}.xo.{m_ - 2}")
                        dve.tensor_copy(PT_sb[L][:, m_ % 2, 1, :], bank(jn)).then_inc(emptied["dve"], 1)
                    t = m_ + 1
                    if 0 <= t < NT:
                        wait_emptied(dve, f"{L}.xl.{t}.1")
                        if t >= 3:
                            dve.wait_ge(x_prob, L * NT + t - 2)
                        dve.reciprocal(soft[:, t % 3, 2, :], soft[:, t % 3, 1, :]).then_inc(x_inv, 1)
                    t = m_ + 2
                    if t < NT:
                        wait_filled(dve, f"{L}.xl.{t}.1")
                        if t >= 3:
                            wait_emptied(dve, f"{L}.xl.{t - 3}.1")
                        for par in range(2):
                            nm = soft[:, t % 3, 0, :].rearrange("p (a b) -> p b a", b=2)[:, par, :]
                            ins = dve.tensor_reduce(nm, bank(f"{L}.xl.{t}.{par}").rearrange("p (a n) -> p a n", a=2), AX.X, ALU.max, negate=True)
                            if par:
                                ins.then_inc(x_max, 1)
                    if m_ >= 0:
                        jn = f"{L}.xo.{m_}"
                        wait_filled(dve, jn)
                        dve.tensor_copy(mix[:, 6:8, m_ * P:(m_ + 1) * P], bank(jn)[:, 0:2 * P].rearrange("p (a n) -> p a n", a=2))\
                           .then_inc(emptied["dve"], 1)
                if L == 1:
                    dve.wait_ge(ld["bias"], 16)
                    gs = attention_groups()
                    for m_ in range(-2, len(gs) + 1):
                        if 0 <= m_ < len(gs):
                            qb, g = gs[m_]
                            for s in range(qb + 1):
                                if pt_reader(qb, g, s) == "dve":
                                    jn = f"1.pt.{qb}.{g}.{s}"
                                    wait_filled(dve, jn)
                                    dve.tensor_copy(PT_sb[1][:, m_ % 2, s, :], bank(jn)).then_inc(emptied["dve"], 1)
                        if m_ >= 1:
                            qb, g = gs[m_ - 1]
                            jn = f"1.uv.{qb}.{g}"
                            wait_filled(dve, jn)
                            dve.tensor_copy(mix[:, 2 * g:2 * g + 2, qb * P:(qb + 1) * P], bank(jn)[:, 0:2 * P].rearrange("p (a n) -> p a n", a=2))\
                               .then_inc(emptied["dve"], 1)
                        n = m_ + 1
                        if 0 <= n < len(gs):
                            dve.wait_ge(l_exp, 4 * (n + 1))
                            if n >= 3:
                                dve.wait_ge(l_prob, n - 2)
                            dve.reciprocal(soft[:, n % 3, 2, :], soft[:, n % 3, 1, :]).then_inc(l_inv, 1)
                        n = m_ + 2
                        if n < len(gs):
                            qb, g = gs[n]
                            w = (qb + 1) * P
                            if n >= 3:
                                pq, pg = gs[n - 3]
                                wait_filled(dve, f"1.pt.{pq}.{pg}.{pq}")
                            elif n == 0:
                                wait_filled(dve, f"1.xp.{NT - 1}.1")
                            for h in range(4):
                                jn = f"1.l.{qb}.{g}.{h}"
                                wait_filled(dve, jn)
                                dve.tensor_tensor_reduce(out=P_sb[:, n % 3, h, 0:w], in0=bank(jn)[:, 0:w],
                                                         in1=T_all[:, 4 * g + h, S - w:S], scale=1.0, scalar=-3.0e38,
                                                         op0=ALU.add, op1=ALU.max, accum_out=soft[:, n % 3, 3, h:h + 1])\
                                   .then_inc(emptied["dve"], 1)
                            wait_emptied(dve, f"1.l.{qb}.{g}.3")
                            dve.tensor_scalar(soft[:, n % 3, 0, :], soft[:, n % 3, 3, :], -1.0, None, ALU.mult).then_inc(l_max, 1)
                rt = route_area
                lg = memKT[:, 0].rearrange("p a b -> p (a b)")[:, 0:NT * R].rearrange("p (t r) -> p t r", t=NT)
                grp, exl = lg[:, :, 0:NG], lg[:, :, NG:R]
                for what, t in out_order():
                    if what == "out":
                        for h in range(2):
                            jn = f"{L}.out.{t}.{h}"
                            wait_filled(dve, jn)
                            xt_ = x[:, t, h * 512:(h + 1) * 512]
                            dve.tensor_tensor(xt_, bank(jn), xt_, ALU.add).then_inc(emptied["dve"], 1)
                        rows_normalise(L, "ffn", (t,), lambda t: x[:, t, :], lambda t: xn_ffn[:, t, :])
                    elif what == "fT":
                        for h in range(2):
                            spread_gain(f"{L}.fT.{t}.{h}", xT[:, 4 * h:4 * h + 4, t * P:(t + 1) * P], 3 * L + 2, h, P)
                    else:
                        wait_filled(dve, f"{L}.route.{t}")
                        dve.tensor_tensor(lg[:, t, :], bank(f"{L}.route.{t}")[:, 0:R], b_route[:, L, :], ALU.add)\
                           .then_inc(emptied["dve"], 1)
                wait_emptied(dve, f"{L}.route.3")
                gm = small[:, 218:218 + NT]
                line.link(dve.tensor_reduce(gm, grp, AX.X, ALU.max))
                eg = small[:, 160:160 + NT * NG].rearrange("p (t g) -> p t g", t=NT)
                gmb = gm.unsqueeze(2).to_broadcast([P, NT, NG])
                dve.tensor_tensor(eg, grp, gmb, ALU.subtract).then_inc(r_diff, 1)
                first = rt[:, 160:160 + NT * NG].rearrange("p (t g) -> p t g", t=NT)
                line.link(dve.tensor_tensor(first, grp, gmb, ALU.is_equal))
                line.link(dve.tensor_tensor(first, first, rank_w[:].unsqueeze(1).to_broadcast([P, NT, NG]), ALU.mult))
                fm = small[:, 222:222 + NT]
                line.link(dve.tensor_reduce(fm, first, AX.X, ALU.max))
                line.link(dve.tensor_tensor(first, first, fm.unsqueeze(2).to_broadcast([P, NT, NG]), ALU.is_equal))
                line.link(dve.tensor_scalar(first, first, -BIG, BIG, ALU.mult, ALU.add))
                e4 = exl.rearrange("p t (g e) -> p t g e", g=NG)
                eall = rt[:, 192:192 + NT * NE].rearrange("p (t e) -> p t e", t=NT)
                for t in range(NT):
                    line.step(dve.tensor_tensor(eall[:, t, :].rearrange("p (g e) -> p g e", g=NG), e4[:, t],
                                                first[:, t, :].unsqueeze(2).to_broadcast([P, NG, EG]), ALU.add))
                line.settle()
                for t in range(NT):
                    line.step(dve.max(v8[:, t, :], eall[:, t, :]))
                line.settle()
                for t in range(NT):
                    line.step(dve.max_index(i8[:, t, :], v8[:, t, :], eall[:, t, :]))
                line.settle()
                e2 = small[:, 184:184 + NT]
                dve.tensor_tensor(e2, v8[:, :, 1], v8[:, :, 0], ALU.subtract).then_inc(r_diff, 1)
                idf = small[:, 226:226 + 2 * NT].rearrange("p (t k) -> p t k", k=2)
                line.link(dve.tensor_copy(idf, i8[:, :, 0:2]))
                oh = [rt[:, 320 + 128 * k:448 + 128 * k].rearrange("p (t e) -> p t e", t=NT) for k in range(2)]
                iob = iota_e[:].unsqueeze(1).to_broadcast([P, NT, NE])
                for k in range(2):
                    line.step(dve.tensor_tensor(oh[k], iob, idf[:, :, k:k + 1].to_broadcast([P, NT, NE]), ALU.is_equal))
                line.settle()
                dve.tensor_tensor(choice[:], oh[0], oh[1], ALU.add).then_inc(chosen, 1)
                dve.wait_ge(r_exp, 2 * L + 1)
                sg, g1, g2 = (small[:, 234 + 4 * q:238 + 4 * q] for q in range(3))
                line.link(dve.tensor_reduce(sg, eg, AX.X, ALU.add))
                dve.wait_ge(r_exp, 2 * L + 2)
                line.link(dve.tensor_scalar(g1, e2, 1.0, None, ALU.add))
                line.link(dve.tensor_tensor(g1, g1, sg, ALU.mult))
                line.link(dve.reciprocal(g1, g1))
                if L:
                    dve.wait_ge(scattered, 16 * 2 * NT * L)
                line.step(dve.tensor_copy(pay[:, 0, :, 1], g1))
                line.step(dve.tensor_tensor(pay[:, 1, :, 1], g1, e2, ALU.mult))
                line.settle()
                line.link(dve.tensor_copy(pay_t[:, :, :, 1], pay[:, :, :, 1]))
                for k in range(2):
                    line.step(dve.tensor_tensor(expert_pay[:, k], oh[k].unsqueeze(2).to_broadcast([P, NT, 2, NE]),
                                                pay_t[:, k].unsqueeze(3).to_broadcast([P, NT, 2, NE]), ALU.mult))
                wait_filled(dve, f"{L}.rank")
                ranks = bank(f"{L}.rank")[:, 0:NT * NE].rearrange("p (t e) -> p t e", t=NT)
                place = [small[:, 16 + NT * k:16 + NT * (k + 1)] for k in range(2)]
                hit = [rt[:, 576:704].rearrange("p (t e) -> p t e", t=NT), rt[:, 1024:1152].rearrange("p (t e) -> p t e", t=NT)]
                for k in range(2):
                    line.step(dve.tensor_tensor(hit[k], oh[k], ranks, ALU.mult))
                line.settle()
                for k in range(2):
                    line.step(dve.tensor_reduce(place[k], hit[k], AX.X, ALU.add))
                line.settle()
                for k, c in ((0, 0), (0, 1), (1, 0), (1, 1)):
                    ins = dve.tensor_tensor(place_hot[:, k, :, c], iota_tok[:, 0:CAP].unsqueeze(1).to_broadcast([P, NT, CAP]),
                                            place[k].unsqueeze(2).to_broadcast([P, NT, CAP]), ALU.is_equal)
                    if (k, c) != (1, 1):
                        line.link(ins)
                    else:
                        ins.then_inc(placed, 1)
                dve.tensor_copy(rt[:, 960:960 + NE], bank(f"{L}.rank")[:, NT * NE:(NT + 1) * NE]).then_inc(emptied["dve"], 1)
                row = small[:, 24:24 + 2 * NT].rearrange("p (k t) -> p k t", k=2)
                for k in range(2):
                    line.step(dve.scalar_tensor_tensor(out=row[:, k, :], in0=place[k], scalar=float(NE), in1=idf[:, :, k],
                                                       op0=ALU.mult, op1=ALU.add))
                line.settle()
                dve.tensor_copy(dest[:], row).then_inc(routed, 1)
                wait_filled(dve, f"{L}.table")
                tb = bank(f"{L}.table")
                dve.tensor_scalar(tabS[:, 0:NE, 0], tb[:, 0:NE], NOTOK, None, ALU.add).then_inc(tab_ready, 1)
                dve.tensor_copy(tabS[:, 0:NE, 1], tb[:, NE:2 * NE]).then_inc(emptied["dve"], 1)
                wait_emptied(dve, f"{L}.table")
                NO = (NBLK - 1) * NE
                flag, pos = rt[:, 704:704 + NO], rt[:, 1024:1024 + NO]
                f3 = flag.rearrange("p (b e) -> p b e", b=NBLK - 1)
                line.link(dve.tensor_tensor(f3, rt[:, 960:960 + NE].unsqueeze(1).to_broadcast([P, NBLK - 1, NE]), thr[:].unsqueeze(2).to_broadcast([P, NBLK - 1, NE]), ALU.is_gt))
                line.link(dve.tensor_tensor_scan(pos, flag, flag, 0.0, ALU.add, ALU.max))
                if L:
                    dve.wait_ge(moe_done, L)
                line.link(dve.tensor_copy(ov_n[:], pos[0:1, NO - 1:NO]))
                line.link(dve.scalar_tensor_tensor(out=flag, in0=pos, scalar=place1[:, 0:1], in1=flag, op0=ALU.is_equal, op1=ALU.mult))
                p3 = pos.rearrange("p (b e) -> p b e", b=NBLK - 1)
                for q, code in enumerate((iota_e[:].unsqueeze(1).to_broadcast([P, NBLK - 1, NE]),
                                          thr[:].unsqueeze(2).to_broadcast([P, NBLK - 1, NE]))):
                    line.link(dve.tensor_tensor(p3, f3, code, ALU.mult))
                    line.link(dve.tensor_reduce(small[:, 246 + q:247 + q], pos, AX.X, ALU.add))
                line.link(dve.scalar_tensor_tensor(out=small[:, 247:248], in0=small[:, 247:248], scalar=float(NE),
                                                   in1=small[:, 246:247], op0=ALU.mult, op1=ALU.add))
                if L:
                    dve.wait_ge(ov_stored, 16 * L)
                dve.tensor_copy(ov_code[:], small[:, 246:248]).then_inc(chosen, 1)

                def tokens_out(s_psum, val, s_sbuf):
                    dve.wait_ge(s_psum, val)
                    dve.tensor_tensor(tokT, ps[:, 0, :].rearrange("p (k n) -> p k n", k=KD),
                                      gains[:, 3 * L + 2, :].unsqueeze(2).to_broadcast([P, KD, CAP]), ALU.mult).then_inc(s_sbuf, 1)

                def hidden(c, s_):
                    dve.scalar_tensor_tensor(out=h_sb[0:CAP, :], in0=ps[CAP:P, 1, :], scalar=c[CAP:P, 1:2], in1=silu[CAP:P, :],
                                             op0=ALU.mult, op1=ALU.mult).then_inc(s_, 1)

                def one_hot(c, s_):
                    dve.tensor_scalar(onehot, iota_tok[:], c[:, 0:1], None, ALU.is_equal).then_inc(s_, 1)

                def split(q, n):
                    for h in range(2):
                        dve.wait_ge(q["y_high"], n * 2 + (1 + h))
                        dve.tensor_tensor(y_rest[HALF[1 - h], :], ps[HALF[h], 3, :], y_hm[h][HALF[h], :], ALU.subtract)\
                           .then_inc(q["y_rest"], 1)
                    for h in range(2):
                        dve.wait_ge(q["y_mid"], n * 2 + (1 + h))
                        o_ = HALF[1 - h]
                        dve.tensor_tensor(y_lo[o_, :], y_rest[o_, :], y_hm[h][o_, :], ALU.subtract).then_inc(q["y_low"], 1)

                def add_tile(t, s_):
                    b = 4 + 2 * (t % 2)
                    dve.tensor_tensor(x[:, t, :], ps[:, b:b + 2, :].rearrange("p a n -> p (a n)"), x[:, t, :], ALU.add).then_inc(s_, 1)

                def add_of(n, ts, started=True):
                    for t in ts:
                        dve.wait_ge(m["c_psum"], n * NT + (t + 1))
                        if started:
                            dve.wait_ge(m["c_added"], n * NT + (t - 3))
                        add_tile(t, m["c_added"])

                def expert(n, e, first=False, second=False):
                    dve.tensor_copy(cur[:], tabS[:, e, :] if isinstance(e, int) else
                                    tabS[:, bass.ds(e, 1), :].rearrange("p a b -> p (a b)")).then_inc(cur_ready, 1)
                    dve.wait_ge(cur_ready, n + 1)
                    dve.wait_ge(m["gu_psum"], n + 1)
                    dve.wait_ge(m["silu_done"], n + 1)
                    hidden(cur[:], m["h_done"])
                    if not first:
                        add_of(n + (-1), (0, 1), not second)
                    tokens_out(m["xt_psum"], n + (L + 2), m["xt_sbuf"])
                    if not first:
                        add_of(n + (-1), (2, 3), not second)
                    one_hot(cur[:], m["g_done"])
                    split(m, n)

                n0 = NE * L
                wait_emptied(dve, f"{L}.out.{NT - 1}.1")
                tokens_out(m["xt_psum"], n0 + (L + 1), m["xt_sbuf"])
                expert(n0, 0, first=True)
                expert(n0 + 1, 1, second=L == 0)
                with dve.Fori(2, NE) as e:
                    expert(e + n0, e)
                add_of(n0 + NE - 1, range(NT))
                o = ov[L]
                dve.wait_ge(ld["ovl"], 16 * (L + 1))
                n_ov = dve.value_load(ov_n[0:1, 0:1], min_val=0, max_val=OVMAX)
                dve.wait_ge(m["c_added"], NT * (n0 + NE))
                with dve.If(n_ov > 0):
                    with dve.Fori(0, n_ov) as i:
                        tokens_out(o["xt_psum"], i + 1, o["xt_sbuf"])
                        dve.wait_ge(o["cur"], i * 32 + 32)
                        one_hot(ov_cur[:, :], o["g_done"])
                        dve.wait_ge(o["gu_psum"], i + 1)
                        dve.wait_ge(o["silu_done"], i + 1)
                        hidden(ov_cur[:, :], o["h_done"])
                        split(o, i)
                        for t in range(NT):
                            dve.wait_ge(o["c_psum"], i * NT + (t + 1))
                            add_tile(t, o["c_added"])
                        wait_alone(dve, o["c_added"], i * NT + NT)
                dve.memset(small[:, 252:253], 0.0).then_inc(moe_done, 1)


_INS = ["x", "mem", "norm_mix", "norm_ffn", "mem_norm", "w_mem_kv", "xq_norm", "xk_norm", "w_out", "lru_w_in", "lru_conv_w",
        "lru_conv_b", "lru_w_a", "lru_b_a", "lru_w_x", "lru_b_x", "lru_lambda", "dsa_w_in", "dsa_q_norm", "dsa_k_norm",
        "dsa_w_uv", "rel_bias", "moe_w_group", "moe_b_group", "moe_w_router", "moe_b_router", "moe_w_gate", "moe_w_up",
        "moe_w_down"]


def kernel(**inputs):
    import concourse.bacc as bacc
    from concourse.bass_utils import run_bass_kernel_spmd

    nc = bacc.Bacc("TRN2", target_bir_lowering=False, num_devices=1)
    arrays, aps = {}, {}
    for name in _INS:
        v = np.ascontiguousarray(inputs[name])
        arrays[f"in_{name}"] = v
        aps[name] = nc.dram_tensor(f"in_{name}", v.shape, mybir.dt.from_np(v.dtype), kind="ExternalInput").ap()
    out = nc.dram_tensor("out", (1, S, D), F32, kind="ExternalOutput").ap()
    hybrid_trunk(nc, aps, out)
    r = run_bass_kernel_spmd(nc, [arrays], core_ids=[0])
    return r.results[0]["out"]
```
